# Optimizing a Trainium2 kernel written in Bass

```python
import math
import jax
import jax.numpy as jnp
from jax import lax
import numpy as np

D_MODEL = 1024
BATCH = 1
SEQ = 2048
DEPTH = 1
DEC_BATCH = 8
DEC_SEQ = 4
PAST_LEN = 2048
PAGE_SIZE = 128

D_MIX = D_MODEL
N_GROUPS = 4
GROUP_W = D_MIX // N_GROUPS
HEAD_DIM = 64
FOX_HEADS = GROUP_W // HEAD_DIM
HGRN_HEADS = GROUP_W // HEAD_DIM
HGRN_CHUNK = 64
NSA_HEADS = GROUP_W // HEAD_DIM
NSA_KV_ROWS = 6
NSA_CMP_BLOCK = 32
NSA_SEL_BLOCK = 64
NSA_TOPK = 16
NSA_WINDOW = 512
LRU_WIDTH = GROUP_W
LRU_BLOCKS = 4
LRU_CONV = 4
LRU_C = 8.0
MEM_LEN = 256
XA_HEADS = 4
XA_HEAD_DIM = 64
D_FF = 4 * D_MODEL
Q_BLOCK = 128
N_NORMS = 6
EPS = 1e-6
NEG_BIG = -1e30
SEL_FORCED = 1e9
SEL_INVALID = -1e9
LB_FLOOR = 1e-30
SPLIT_SIZES = (GROUP_W, GROUP_W, GROUP_W, FOX_HEADS,
               GROUP_W, GROUP_W, GROUP_W, GROUP_W,
               GROUP_W, NSA_KV_ROWS * HEAD_DIM, 3 * NSA_HEADS,
               LRU_WIDTH, LRU_WIDTH)
D_PROJ = sum(SPLIT_SIZES)

kernel_name = 'hymba_fox_hgrn2_nsa_rglru_step'

F32 = jnp.float32

def _rms(x, g):
    xf = x.astype(F32)
    y = xf * lax.rsqrt(jnp.mean(xf * xf, axis=-1, keepdims=True) + EPS)
    return (y * g.astype(F32)).astype(x.dtype)

def _split_proj(z):
    idx = np.cumsum(SPLIT_SIZES)[:-1].tolist()
    return jnp.split(z, idx, axis=-1)

def _masked_softmax(s, mask):
    s = jnp.where(mask, s.astype(F32), NEG_BIG)
    m = jnp.max(s, axis=-1, keepdims=True)
    e = jnp.where(mask, jnp.exp(s - m), 0.0)
    d = jnp.sum(e, axis=-1, keepdims=True)
    return e / jnp.where(d > 0, d, 1.0)

def _to_blocks(a, nb):
    return jnp.moveaxis(a.reshape((a.shape[0], nb, Q_BLOCK) + a.shape[2:]), 1, 0)

def _from_blocks(a):
    a = jnp.moveaxis(a, 0, 1)
    return a.reshape((a.shape[0], a.shape[1] * a.shape[2]) + a.shape[3:])

def _fox_attend(q, q_pos, cq, k, v, ck):
    s = jnp.einsum('bqhd,bshd->bhqs', q, k).astype(F32) * (HEAD_DIM ** -0.5)
    s = s + jnp.transpose(cq, (0, 2, 1))[..., None] - jnp.transpose(ck, (0, 2, 1))[:, :, None, :]
    mask = jnp.arange(k.shape[1])[None, :] <= q_pos[:, None]
    p = _masked_softmax(s, mask)
    return jnp.einsum('bhqs,bshd->bqhd', p.astype(v.dtype), v)

def _fox_prompt(q, k, v, logf):
    B, L = q.shape[:2]
    nb = L // Q_BLOCK
    c = jnp.cumsum(logf.astype(F32), axis=1)
    pos = jnp.arange(L).reshape(nb, Q_BLOCK)

    def blk(args):
        qb, pb, cb = args
        return _fox_attend(qb, pb, cb, k, v, c)

    return _from_blocks(lax.map(blk, (_to_blocks(q, nb), pos, _to_blocks(c, nb))))

def _fox_sample(q, kv_new, logf_new, past_kv, past_logf):
    P, T = past_kv.shape[1], q.shape[1]
    kv = jnp.concatenate([past_kv.astype(kv_new.dtype), kv_new], axis=1)
    c = jnp.cumsum(jnp.concatenate([past_logf.astype(F32), logf_new], axis=1), axis=1)
    pos = P + jnp.arange(T)
    return _fox_attend(q, pos, c[:, P:], kv[:, :, 0], kv[:, :, 1], c)

def _gla_chunked(q, k, v, log_f, S0):
    B, L, H, DK = q.shape
    DV = v.shape[-1]
    C = math.gcd(L, HGRN_CHUNK)
    n = L // C

    def chunks(a):
        return jnp.transpose(a.reshape(B, n, C, H, a.shape[-1]), (1, 0, 3, 2, 4))

    causal = jnp.tril(jnp.ones((C, C), dtype=bool))[:, :, None]

    def step(S, inp):
        qc, kc, vc, gc = inp
        b = jnp.cumsum(gc, axis=2)
        rel = b[:, :, :, None, :] - b[:, :, None, :, :]
        decay = jnp.where(causal, jnp.exp(jnp.where(causal, rel, 0.0)), 0.0)
        attn = jnp.einsum('bhtk,bhsk,bhtsk->bhts', qc, kc, decay)
        o = (jnp.einsum('bhts,bhsv->bhtv', attn, vc)
             + jnp.einsum('bhtk,bhkv->bhtv', qc * jnp.exp(b), S))
        b_last = b[:, :, -1, :]
        S = (jnp.exp(b_last)[..., None] * S
             + jnp.einsum('bhsk,bhsv->bhkv', kc * jnp.exp(b_last[:, :, None, :] - b), vc))
        return S, o

    S, o = lax.scan(step, S0, (chunks(q), chunks(k), chunks(v), chunks(log_f)))
    return jnp.transpose(o, (1, 0, 3, 2, 4)).reshape(B, L, H, DV), S

def _hgrn2(q_raw, f_raw, i_raw, g_raw, lb, gain, S0):
    B, L, _ = q_raw.shape
    heads = lambda a: a.reshape(B, L, HGRN_HEADS, HEAD_DIM)
    q = jax.nn.silu(heads(q_raw)).astype(F32)
    z = heads(f_raw).astype(F32)
    lbh = lb.reshape(HGRN_HEADS, HEAD_DIM).astype(F32)
    log_f = jnp.logaddexp(jnp.log1p(-lbh) + jax.nn.log_sigmoid(z), jnp.log(jnp.maximum(lbh, LB_FLOOR)))
    k = (1.0 - lbh) * jax.nn.sigmoid(-z)
    o, S = _gla_chunked(q, k, heads(i_raw).astype(F32), log_f, S0.astype(F32))
    o = _rms(o, gain.reshape(HGRN_HEADS, HEAD_DIM)).reshape(B, L, GROUP_W)
    return o.astype(q_raw.dtype) * jax.nn.silu(g_raw), S

def _nsa_compress(kc, vc, w_cmp):
    B, L, D = kc.shape
    N = L // NSA_CMP_BLOCK
    blocks = lambda a: a[:, :N * NSA_CMP_BLOCK].reshape(B, N, NSA_CMP_BLOCK, D)
    kcmp = jnp.einsum('bnjd,jd->bnd', blocks(kc), w_cmp[0])
    vcmp = jnp.einsum('bnjd,jd->bnd', blocks(vc), w_cmp[1])
    cmp_end = (jnp.arange(N) + 1) * NSA_CMP_BLOCK - 1
    return kcmp, vcmp, cmp_end

def _sel_blocks(a):
    B, L, D = a.shape
    NS = -(-L // NSA_SEL_BLOCK)
    a = jnp.pad(a, ((0, 0), (0, NS * NSA_SEL_BLOCK - L), (0, 0)))
    return a.reshape(B, NS, NSA_SEL_BLOCK, D)

def _nsa_core(q, pos, gates, kcmp, vcmp, cmp_end, ks_blk, vs_blk, kw, vw, kw_pos):
    B, Q, H, D = q.shape
    N, NS = kcmp.shape[1], ks_blk.shape[1]
    scale = D ** -0.5
    s_c = jnp.einsum('bqhd,bnd->bhqn', q, kcmp) * scale
    p_c = _masked_softmax(s_c, cmp_end[None, :] <= pos[:, None])
    o_c = jnp.einsum('bhqn,bnd->bqhd', p_c.astype(q.dtype), vcmp)
    ratio = NSA_SEL_BLOCK // NSA_CMP_BLOCK
    imp = jnp.sum(p_c, axis=1)
    imp = jnp.pad(imp, ((0, 0), (0, 0), (0, NS * ratio - N))).reshape(B, Q, NS, ratio).sum(-1)
    blk = jnp.arange(NS)
    forced = (blk[None, :] == pos[:, None] // NSA_SEL_BLOCK) | (blk[None, :] == 0)
    causal = blk[None, :] * NSA_SEL_BLOCK <= pos[:, None]
    imp = jnp.where(forced, SEL_FORCED, jnp.where(causal, imp, SEL_INVALID))
    n_top = min(NSA_TOPK, NS)
    top_val, top_idx = lax.top_k(imp, n_top)
    ks_g = jax.vmap(lambda kb, ix: kb[ix])(ks_blk, top_idx)
    vs_g = jax.vmap(lambda vb, ix: vb[ix])(vs_blk, top_idx)
    tok = top_idx[..., None] * NSA_SEL_BLOCK + jnp.arange(NSA_SEL_BLOCK)
    m_s = (top_val[..., None] >= 0.0) & (tok <= pos[None, :, None, None])
    s_s = jnp.einsum('bqhd,bqkjd->bhqkj', q, ks_g) * scale
    p_s = _masked_softmax(s_s.reshape(B, H, Q, -1), m_s.reshape(B, 1, Q, -1))
    o_s = jnp.einsum('bhqm,bqmd->bqhd', p_s.astype(q.dtype), vs_g.reshape(B, Q, -1, D))
    s_w = jnp.einsum('bqhd,bkd->bhqk', q, kw) * scale
    dist = pos[:, None] - kw_pos[None, :]
    p_w = _masked_softmax(s_w, (dist >= 0) & (dist < NSA_WINDOW) & (kw_pos[None, :] >= 0))
    o_w = jnp.einsum('bhqk,bkd->bqhd', p_w.astype(q.dtype), vw)
    return gates[..., 0:1] * o_c + gates[..., 1:2] * o_s + gates[..., 2:3] * o_w

def _nsa_prompt(q, kv6, gates, w_cmp):
    B, L = q.shape[:2]
    nb = L // Q_BLOCK
    kcmp, vcmp, cmp_end = _nsa_compress(kv6[:, :, 0], kv6[:, :, 1], w_cmp)
    ks_blk, vs_blk = _sel_blocks(kv6[:, :, 2]), _sel_blocks(kv6[:, :, 3])
    pad = ((0, 0), (NSA_WINDOW, 0), (0, 0))
    kw_pad, vw_pad = jnp.pad(kv6[:, :, 4], pad), jnp.pad(kv6[:, :, 5], pad)
    pos = jnp.arange(L).reshape(nb, Q_BLOCK)

    def blk(args):
        qb, pb, gb = args
        start = pb[0]
        kw = lax.dynamic_slice_in_dim(kw_pad, start, NSA_WINDOW + Q_BLOCK, axis=1)
        vw = lax.dynamic_slice_in_dim(vw_pad, start, NSA_WINDOW + Q_BLOCK, axis=1)
        kw_pos = start - NSA_WINDOW + jnp.arange(NSA_WINDOW + Q_BLOCK)
        return _nsa_core(qb, pb, gb, kcmp, vcmp, cmp_end, ks_blk, vs_blk, kw, vw, kw_pos)

    return _from_blocks(lax.map(blk, (_to_blocks(q, nb), pos, _to_blocks(gates, nb))))

def _nsa_sample(q, kv6, gates, w_cmp, past_kv4, win_buf):
    P, T, WB = past_kv4.shape[1], q.shape[1], win_buf.shape[1]
    full = jnp.concatenate([past_kv4.astype(kv6.dtype), kv6[:, :, :4]], axis=1)
    kcmp, vcmp, cmp_end = _nsa_compress(full[:, :, 0], full[:, :, 1], w_cmp)
    ks_blk, vs_blk = _sel_blocks(full[:, :, 2]), _sel_blocks(full[:, :, 3])
    win = jnp.concatenate([win_buf.astype(kv6.dtype), kv6[:, :, 4:]], axis=1)
    kw_pos = P - WB + jnp.arange(WB + T)
    pos = P + jnp.arange(T)
    o = _nsa_core(q, pos, gates, kcmp, vcmp, cmp_end, ks_blk, vs_blk, win[:, :, 0], win[:, :, 1], kw_pos)
    return o, win[:, -WB:]

def _lin_comb(e1, e2):
    return e1[0] * e2[0], e2[0] * e1[1] + e2[1]

def _rglru(u_raw, gate, conv_buf, h0, W, l):
    B, L, _ = u_raw.shape
    cw = W['lru_conv_w'][l]
    xp = jnp.concatenate([conv_buf.astype(u_raw.dtype), u_raw], axis=1)
    u = W['lru_conv_b'][l] + xp[:, 0:L] * cw[0]
    for j in range(1, LRU_CONV):
        u = u + xp[:, j:j + L] * cw[j]
    ub = u.reshape(B, L, LRU_BLOCKS, LRU_WIDTH // LRU_BLOCKS)
    r = jax.nn.sigmoid(jnp.einsum('blnc,ncd->blnd', ub, W['lru_wa'][l]).reshape(B, L, LRU_WIDTH) + W['lru_ba'][l])
    i = jax.nn.sigmoid(jnp.einsum('blnc,ncd->blnd', ub, W['lru_wx'][l]).reshape(B, L, LRU_WIDTH) + W['lru_bx'][l])
    log_a = -LRU_C * r.astype(F32) * jax.nn.softplus(-W['lru_lambda'][l].astype(F32))
    a = jnp.exp(log_a)
    b = jnp.sqrt(-jnp.expm1(2.0 * log_a)) * (i * u).astype(F32)
    b = b.at[:, 0].add(a[:, 0] * h0.astype(F32))
    _, h = lax.associative_scan(_lin_comb, (a, b), axis=1)
    y = h.astype(u_raw.dtype) * jax.nn.gelu(gate)
    return y, xp[:, L:], h[:, -1]

def _project(x, W, l):
    h = _rms(x, W['norms'][l, 0])
    return _split_proj(h @ W['w_in'][l])

def _mix_residual(x, o_a, o_b, o_c, o_d, W, l):
    B, L, _ = x.shape
    gm = W['g_mix'][l]
    groups = jnp.concatenate([
        _rms(o_a.reshape(B, L, GROUP_W), gm[:GROUP_W]),
        o_b.astype(x.dtype),
        _rms(o_c.reshape(B, L, GROUP_W), gm[2 * GROUP_W:3 * GROUP_W]),
        _rms(o_d, gm[3 * GROUP_W:])], axis=-1)
    y = groups @ W['w_out'][l]
    return x + _rms(y, W['norms'][l, 1])

def _mem_kv(mem, W, l):
    m = _rms(mem, W['g_mem'][l])
    return (m @ W['xa_wkv'][l]).reshape(mem.shape[0], mem.shape[1], 2, XA_HEADS, XA_HEAD_DIM)

def _cross_and_ffn(x, xa_kv, W, l):
    B, L, _ = x.shape
    h = _rms(x, W['norms'][l, 2])
    q = (h @ W['xa_wq'][l]).reshape(B, L, XA_HEADS, XA_HEAD_DIM)
    kv = xa_kv.astype(x.dtype)
    s = jnp.einsum('bqhd,bmhd->bhqm', q, kv[:, :, 0]).astype(F32) * (XA_HEAD_DIM ** -0.5)
    p = jax.nn.softmax(s, axis=-1)
    o = jnp.einsum('bhqm,bmhd->bqhd', p.astype(x.dtype), kv[:, :, 1]).reshape(B, L, -1) @ W['xa_wo'][l]
    x = x + _rms(o, W['norms'][l, 3])
    h = _rms(x, W['norms'][l, 4])
    f = jnp.square(jax.nn.relu(h @ W['w_ff1'][l])) @ W['w_ff2'][l]
    return x + _rms(f, W['norms'][l, 5])

def _prompt_layer(x, mem, W, l, lb):
    B, L, _ = x.shape
    fq, fk, fv, ff, hq, hf, hi, hg, nq, nkv, ng, ux, ug = _project(x, W, l)
    heads = lambda a: a.reshape(B, L, -1, HEAD_DIM)
    fox_logf = jax.nn.log_sigmoid((ff + W['b_fox_f'][l]).astype(F32))
    fox_kv = jnp.stack([heads(fk), heads(fv)], axis=2)
    o_a = _fox_prompt(heads(fq), fox_kv[:, :, 0], fox_kv[:, :, 1], fox_logf)
    S0 = jnp.zeros((B, HGRN_HEADS, HEAD_DIM, HEAD_DIM), F32)
    o_b, S = _hgrn2(hq, hf, hi, hg, lb, W['g_mix'][l, GROUP_W:2 * GROUP_W], S0)
    nkv = nkv.reshape(B, L, NSA_KV_ROWS, HEAD_DIM)
    gates = jax.nn.sigmoid(ng.reshape(B, L, NSA_HEADS, 3))
    o_c = _nsa_prompt(heads(nq), nkv, gates, W['nsa_cmp_w'][l])
    wb = min(NSA_WINDOW, L)
    nsa_win = nkv[:, L - wb:, 4:]
    buf0 = jnp.zeros((B, LRU_CONV - 1, LRU_WIDTH), x.dtype)
    h0 = jnp.zeros((B, LRU_WIDTH), F32)
    o_d, conv_buf, h_last = _rglru(ux, ug, buf0, h0, W, l)
    x = _mix_residual(x, o_a, o_b, o_c, o_d, W, l)
    xa_kv = _mem_kv(mem, W, l)
    x = _cross_and_ffn(x, xa_kv, W, l)
    return x, (fox_kv, fox_logf, nkv[:, :, :4], nsa_win, S, h_last, conv_buf, xa_kv)

def _sample_layer(x, W, l, lb, page_table, fox_kv_pages, fox_logf_pages, nsa_pages,
                  win_buf, S0, h0, conv_buf, xa_kv):
    B, T, _ = x.shape
    fq, fk, fv, ff, hq, hf, hi, hg, nq, nkv, ng, ux, ug = _project(x, W, l)
    heads = lambda a: a.reshape(B, T, -1, HEAD_DIM)
    fox_logf = jax.nn.log_sigmoid((ff + W['b_fox_f'][l]).astype(F32))
    fox_kv = jnp.stack([heads(fk), heads(fv)], axis=2)
    past_kv = fox_kv_pages[page_table].reshape((B, -1) + fox_kv_pages.shape[2:])
    past_logf = fox_logf_pages[page_table].reshape(B, -1, FOX_HEADS)
    o_a = _fox_sample(heads(fq), fox_kv, fox_logf, past_kv, past_logf)
    o_b, S = _hgrn2(hq, hf, hi, hg, lb, W['g_mix'][l, GROUP_W:2 * GROUP_W], S0)
    nkv = nkv.reshape(B, T, NSA_KV_ROWS, HEAD_DIM)
    gates = jax.nn.sigmoid(ng.reshape(B, T, NSA_HEADS, 3))
    past_nsa = nsa_pages[page_table].reshape((B, -1) + nsa_pages.shape[2:])
    o_c, new_win = _nsa_sample(heads(nq), nkv, gates, W['nsa_cmp_w'][l], past_nsa, win_buf)
    o_d, new_conv, h_last = _rglru(ux, ug, conv_buf, h0, W, l)
    x = _mix_residual(x, o_a, o_b, o_c, o_d, W, l)
    x = _cross_and_ffn(x, xa_kv, W, l)
    return x, (fox_kv, fox_logf, nkv[:, :, :4], new_win, S, h_last, new_conv)

def _stack(outs, i):
    return jnp.stack([o[i] for o in outs], axis=0)

def setup_inputs(seed: int = 0) -> dict:
    key = jax.random.key(seed)
    k = jax.random.split(key, 32)

    def nrm(i, shape, scale=1.0):
        return scale * jax.random.normal(k[i], shape, F32)

    n_pages = PAST_LEN // PAGE_SIZE
    n_phys = (DEC_BATCH * n_pages * 5) // 4
    win = min(NSA_WINDOW, PAST_LEN)
    bs = LRU_WIDTH // LRU_BLOCKS
    page_table = jax.random.permutation(k[0], n_phys)[:DEC_BATCH * n_pages].reshape(DEC_BATCH, n_pages).astype(jnp.int32)
    a0 = jax.random.uniform(k[1], (DEPTH, LRU_WIDTH), F32, 0.9, 0.999) ** (1.0 / LRU_C)
    return {
        'x_prompt': nrm(2, (BATCH, SEQ, D_MODEL)),
        'mem_prompt': nrm(3, (BATCH, MEM_LEN, D_MODEL)),
        'x_sample': nrm(4, (DEC_BATCH, DEC_SEQ, D_MODEL)),
        'cache_fox_kv': nrm(5, (DEPTH, n_phys, PAGE_SIZE, 2, FOX_HEADS, HEAD_DIM)),
        'cache_fox_logf': jax.nn.log_sigmoid(2.0 + nrm(6, (DEPTH, n_phys, PAGE_SIZE, FOX_HEADS), 0.5)),
        'cache_nsa_kv': nrm(7, (DEPTH, n_phys, PAGE_SIZE, 4, HEAD_DIM)),
        'state_nsa_win': nrm(8, (DEPTH, DEC_BATCH, win, 2, HEAD_DIM)),
        'state_hgrn': nrm(9, (DEPTH, DEC_BATCH, HGRN_HEADS, HEAD_DIM, HEAD_DIM), 0.5),
        'state_lru_h': nrm(10, (DEPTH, DEC_BATCH, LRU_WIDTH), 0.5),
        'state_lru_conv': nrm(11, (DEPTH, DEC_BATCH, LRU_CONV - 1, LRU_WIDTH)),
        'cache_xa_kv': nrm(12, (DEPTH, DEC_BATCH, MEM_LEN, 2, XA_HEADS, XA_HEAD_DIM)),
        'page_table': page_table,
        'w_in': nrm(13, (DEPTH, D_MODEL, D_PROJ), D_MODEL ** -0.5),
        'b_fox_f': 2.0 + nrm(14, (DEPTH, FOX_HEADS), 0.5),
        'hgrn_lower': nrm(15, (DEPTH, HGRN_HEADS * HEAD_DIM), 0.5),
        'nsa_cmp_w': nrm(16, (DEPTH, 2, NSA_CMP_BLOCK, HEAD_DIM), NSA_CMP_BLOCK ** -0.5),
        'lru_conv_w': nrm(17, (DEPTH, LRU_CONV, LRU_WIDTH), LRU_CONV ** -0.5),
        'lru_conv_b': nrm(18, (DEPTH, LRU_WIDTH), 0.01),
        'lru_wa': nrm(19, (DEPTH, LRU_BLOCKS, bs, bs), bs ** -0.5),
        'lru_ba': nrm(20, (DEPTH, LRU_WIDTH), 0.1),
        'lru_wx': nrm(21, (DEPTH, LRU_BLOCKS, bs, bs), bs ** -0.5),
        'lru_bx': nrm(22, (DEPTH, LRU_WIDTH), 0.1),
        'lru_lambda': jnp.log(a0) - jnp.log1p(-a0),
        'g_mix': 1.0 + nrm(23, (DEPTH, D_MIX), 0.05),
        'w_out': nrm(24, (DEPTH, D_MIX, D_MODEL), D_MIX ** -0.5),
        'g_mem': 1.0 + nrm(25, (DEPTH, D_MODEL), 0.05),
        'xa_wq': nrm(26, (DEPTH, D_MODEL, XA_HEADS * XA_HEAD_DIM), D_MODEL ** -0.5),
        'xa_wkv': nrm(27, (DEPTH, D_MODEL, 2 * XA_HEADS * XA_HEAD_DIM), D_MODEL ** -0.5),
        'xa_wo': nrm(28, (DEPTH, XA_HEADS * XA_HEAD_DIM, D_MODEL), (XA_HEADS * XA_HEAD_DIM) ** -0.5),
        'w_ff1': nrm(29, (DEPTH, D_MODEL, D_FF), D_MODEL ** -0.5),
        'w_ff2': nrm(30, (DEPTH, D_FF, D_MODEL), D_FF ** -0.5),
        'norms': 1.0 + nrm(31, (DEPTH, N_NORMS, D_MODEL), 0.05),
    }

def reference(x_prompt, mem_prompt, x_sample, cache_fox_kv, cache_fox_logf, cache_nsa_kv,
              state_nsa_win, state_hgrn, state_lru_h, state_lru_conv, cache_xa_kv, page_table,
              w_in, b_fox_f, hgrn_lower, nsa_cmp_w, lru_conv_w, lru_conv_b, lru_wa, lru_ba,
              lru_wx, lru_bx, lru_lambda, g_mix, w_out, g_mem, xa_wq, xa_wkv, xa_wo,
              w_ff1, w_ff2, norms):
    W = dict(w_in=w_in, b_fox_f=b_fox_f, nsa_cmp_w=nsa_cmp_w, lru_conv_w=lru_conv_w,
             lru_conv_b=lru_conv_b, lru_wa=lru_wa, lru_ba=lru_ba, lru_wx=lru_wx, lru_bx=lru_bx,
             lru_lambda=lru_lambda, g_mix=g_mix, w_out=w_out, g_mem=g_mem, xa_wq=xa_wq,
             xa_wkv=xa_wkv, xa_wo=xa_wo, w_ff1=w_ff1, w_ff2=w_ff2, norms=norms)
    lower = jax.nn.softmax(hgrn_lower.astype(F32), axis=0)
    lbs = jnp.cumsum(lower, axis=0) - lower[0]
    y_p, y_s = x_prompt, x_sample
    p_out, s_out = [], []
    for l in range(DEPTH):
        y_p, po = _prompt_layer(y_p, mem_prompt, W, l, lbs[l])
        y_s, so = _sample_layer(y_s, W, l, lbs[l], page_table, cache_fox_kv[l], cache_fox_logf[l],
                                cache_nsa_kv[l], state_nsa_win[l], state_hgrn[l], state_lru_h[l],
                                state_lru_conv[l], cache_xa_kv[l])
        p_out.append(po)
        s_out.append(so)
    return (y_p, y_s,
            _stack(p_out, 0), _stack(p_out, 1), _stack(p_out, 2), _stack(p_out, 3),
            _stack(p_out, 4), _stack(p_out, 5), _stack(p_out, 6), _stack(p_out, 7),
            _stack(s_out, 0), _stack(s_out, 1), _stack(s_out, 2), _stack(s_out, 3),
            _stack(s_out, 4), _stack(s_out, 5), _stack(s_out, 6))


_drawn_inputs = setup_inputs


def setup_inputs(seed=0):
    import zlib

    import numpy as np

    out = dict(_drawn_inputs(seed))
    spreads = {}
    factors = {}
    for name, (base, spread) in spreads.items():
        noise = np.random.default_rng([zlib.crc32(name.encode()), seed]).standard_normal(out[name].shape)
        drawn = base * np.exp(spread * noise) if base else spread * noise
        out[name] = jnp.asarray(drawn.astype(out[name].dtype))
    for name, factor in factors.items():
        out[name] = (out[name] * factor).astype(out[name].dtype)
    return out
```

```python
from contextlib import ExitStack

import concourse.bass as bass
from concourse import mybir

F32 = mybir.dt.float32
I32 = mybir.dt.int32
ALU = mybir.AluOpType
ACT = mybir.ActivationFunctionType
AX = mybir.AxisListType

D = 1024
L = 2048
NB, NT = 8, 4
TS = NB * NT
T = L + TS
PAGE = 128
NPAGE = 16
PAST = NPAGE * PAGE
HD = 64
NH = 4
GW = 256
FF = 4096
MEM = 256
WIN = 512
P = 128
KC = D // P
TB = 512
NBLK = L // TB
TILES = TB // P
EPS = 1e-6
NEG = -1e30
QSCALE = HD ** -0.5

C_FQ, C_FK, C_FV, C_FF = 0, 256, 512, 768
C_HQ, C_HF, C_HI, C_HG = 772, 1028, 1284, 1540
C_NQ, C_NKV, C_NG, C_UX, C_UG, C_END = 1796, 2052, 2436, 2448, 2704, 2960

R_FQ, R_FK, R_HQ, R_HF, R_HG, R_NQ = 0, 256, 512, 768, 1024, 1280
R_CMP, R_KS, R_KW, R_SM, R_UX, R_UG, R_END = 1536, 1664, 1728, 1792, 1808, 2064, 2320

FEAT = (
    [(C_FQ + P * c, P, R_FQ + P * c, QSCALE) for c in range(2)]
    + [(C_FK + P * c, P, R_FK + P * c, 1.0) for c in range(2)]
    + [(C_HQ + P * c, P, R_HQ + P * c, 1.0) for c in range(2)]
    + [(C_HF + P * c, P, R_HF + P * c, 1.0) for c in range(2)]
    + [(C_HG + P * c, P, R_HG + P * c, 1.0) for c in range(2)]
    + [(C_NQ + P * c, P, R_NQ + P * c, QSCALE) for c in range(2)]
    + [(C_NKV, P, R_CMP, 1.0), (C_NKV + 128, HD, R_KS, 1.0), (C_NKV + 256, HD, R_KW, 1.0)]
    + [(None, 16, R_SM, 1.0)]
    + [(C_UX + P * c, P, R_UX + P * c, 1.0) for c in range(2)]
    + [(C_UG + P * c, P, R_UG + P * c, 1.0) for c in range(2)]
)
NFEAT = len(FEAT)
W_GROUPS = [(C_FK, C_HQ), (C_HI, C_HG), (C_NKV, C_UX), (C_FQ, C_FK), (C_HQ, C_HI), (C_HG, C_NKV), (C_UX, C_END)]


def w_group(column):
    return [k for k, (c0, c1) in enumerate(W_GROUPS) if c0 <= column < c1][0]


G_FOX, G_HGRN, G_CMP, G_SEL, G_WIN, G_LRU, G_END = 0, 256, 512, 768, 1024, 1280, 1536


LN_EXP = "natural_log_exp_and_others"


class Room:

    zeroed = []

    def __init__(self, nc, tag):
        self.nc, self.tag, self.ctx, self.owned = nc, tag, ExitStack(), []

    def __enter__(self):
        self.ctx.__enter__()
        return self

    def __exit__(self, *a):
        done = self.ctx.__exit__(*a)
        for old in Room.zeroed:
            self.nc.release_semaphore(old)
        for own in self.owned:
            self.nc.gpsimd.sem_clear(own)
        Room.zeroed = self.owned
        return done

    def sb(self, name, shape, dt=F32):
        return self.ctx.enter_context(self.nc.sbuf_tensor(f"{self.tag}_{name}", shape, dt))

    def ps(self, name, shape, dt=F32):
        return self.ctx.enter_context(self.nc.psum_tensor(f"{self.tag}_{name}", shape, dt))

    def sem(self, name):
        self.owned.append(self.nc.alloc_semaphore(f"{self.tag}_{name}"))
        return self.owned[-1]

    def pool_sem(self, name):
        return self.nc.alloc_semaphore(f"{self.tag}_{name}")

    def pool_sems(self, name, n):
        return [self.pool_sem(f"{name}{k}") for k in range(n)]

    def sems(self, name, n):
        return [self.sem(f"{name}{k}") for k in range(n)]

    def block(self):
        return self.ctx.enter_context(self.nc.Block())


def bc(ap, axis, n):
    ap = ap.unsqueeze(axis)
    return ap.broadcast_to([n if k == axis else s for k, s in enumerate(ap.shape)])


def hold(engine, passed, sem, value):
    engine.wait_ge(sem, value)
    engine.sem_inc(passed, 1)


def stage_constants(nc, K):
    with Room(nc, "const") as r:
        made, zeroed = r.sem("made"), r.sem("zeroed")
        block = r.block()

        @block.gpsimd
        def _(pool):
            nc.gpsimd.memset(K["ident"][:], 0.0)
            nc.gpsimd.memset(K["ones"][:], 1.0)
            nc.gpsimd.memset(K["eps"][:], EPS)
            for n in ("tri_kq", "tri_qk", "low_kq", "low_qk"):
                last = nc.gpsimd.memset(K[n][:], 0.0)
            last.then_inc(made, 1)
            pool.wait_ge(made, 1)
            nc.gpsimd.affine_select(out=K["ident"][:], in_=K["ident"][:], pattern=[[-1, P]], base=0,
                                    channel_multiplier=1, compare_op=ALU.not_equal, fill=1.0)
            nc.gpsimd.affine_select(out=K["tri_kq"][:], in_=K["tri_kq"][:], pattern=[[1, P]], base=0,
                                    channel_multiplier=-1, compare_op=ALU.is_ge, fill=NEG)
            nc.gpsimd.affine_select(out=K["tri_qk"][:], in_=K["tri_qk"][:], pattern=[[-1, P]], base=0,
                                    channel_multiplier=1, compare_op=ALU.is_ge, fill=NEG)
            nc.gpsimd.affine_select(out=K["low_kq"][:], in_=K["low_kq"][:], pattern=[[-1, P]], base=0,
                                    channel_multiplier=1, compare_op=ALU.is_gt, fill=NEG)
            nc.gpsimd.affine_select(out=K["low_qk"][:], in_=K["low_qk"][:], pattern=[[1, P]], base=0,
                                    channel_multiplier=-1, compare_op=ALU.is_gt, fill=NEG)


        @block.vector
        def _(dve):
            nc.vector.memset(K["pairones"][:], 0.0).then_inc(zeroed, 1)
            dve.wait_ge(zeroed, 1)
            nc.vector.memset(K["pairones"][0:HD, 0:HD], 1.0)
            nc.vector.memset(K["pairones"][HD:P, HD:P], 1.0)


def stage_project(nc, I, O, S, K):
    with Room(nc, "proj") as r:
        w = r.sb("w", [P, KC, C_END])
        w_small = r.sb("w_small", [P, KC, 16])
        gain = r.sb("gain", [P, KC])
        fbias = r.sb("fbias", [P, NH])
        x = r.sb("x", [P, TILES, D])
        xn = r.sb("xn", [P, TILES, D])
        squares = r.sb("squares", [P, D])
        ss = r.sb("ss", [P, TILES])
        lnss = r.sb("lnss", [P, TILES])
        rstd = r.sb("rstd", [P, TILES])
        hT = r.sb("hT", [P, KC, TB])
        fstage = r.sb("fstage", [P, 4, TB])
        z = r.sb("z", [P, 2, 1152])
        fl = r.sb("fl", [P, 4, TILES * NH])
        p_turn = r.ps("turn", [P, KC * P])
        p_feat = r.ps("feat", [P, 2, TB])
        p_tok = r.ps("tok", [P, 3, TB])

        consts, small_loaded = r.sem("consts"), r.sem("small_loaded")
        w_loaded, passed = r.sems("w_loaded", len(W_GROUPS)), r.sem("passed")
        x_loaded = r.pool_sems("x_loaded", TILES)
        ss_done, ln_done, rstd_done = r.sem("ss_done"), r.sem("ln_done"), r.sem("rstd_done")
        xn_done, turned, hT_done = r.sem("xn_done"), r.sem("turned"), r.sem("hT_done")
        feat_mm, feat_out, feat_stored = r.sem("feat_mm"), r.sem("feat_out"), r.sems("feat_stored", 4)
        tok_mm, tok_out, tok_stored = r.sem("tok_mm"), r.sem("tok_out"), r.sems("tok_stored", 2)
        fz, fabs_, fexp, fln, flog, flog_stored = (r.sem(n) for n in ("fz", "fabs", "fexp", "fln", "flog", "flog_stored"))
        block = r.block()

        def tiles(i):
            return [(t, 4 * i + t) for t in range(TILES)] if not isinstance(i, str) else [(0, 4 * NBLK)]

        def both(engine, body):
            with engine.Fori(0, NBLK) as i:
                body(i, i, P, TILES)
            body(NBLK, None, TS, 1)

        @block.gpsimd
        def _(pool):
            def load(i, blk, rows, nt):
                for t in range(nt):
                    pool.wait_ge(xn_done, 4 * i + t + 1)
                    src = I["x_prompt"][bass.ds(i * TB + t * P, P), :] if blk is not None else I["x_sample"]
                    pool.dma_start(x[0:rows, t, :], src).then_inc(x_loaded[t], 16)
            both(pool, load)

        @block.sync
        def _(sp):
            sp.dma_start(gain[:], I["norms"][0].rearrange("(c p) -> p c", p=P), allow_slow_non_contiguous=True).then_inc(consts, 16)
            sp.dma_start(fbias[:], I["b_fox_f"].partition_broadcast(P)).then_inc(consts, 16)
            for t in range(TILES):
                sp.wait_ge(x_loaded[t], 16)
            for k, (c0, c1) in enumerate(W_GROUPS):
                sp.dma_start(w[:, :, c0:c1], I["w_in"][:, c0:c1].rearrange("(c p) n -> p c n", p=P)).then_inc(w_loaded[k], 16)
            for to, c0, m in ((0, C_FF, 4), (4, C_NG, 12)):
                sp.dma_start(w_small[:, :, to:to + m], I["w_in"][:, c0:c0 + m].rearrange("(c p) n -> p c n", p=P)
                             ).then_inc(small_loaded, 16)

            def store(i, blk, rows, nt):
                width = TB if blk is not None else TS
                for t in range(TILES):
                    if t < nt:
                        hold(sp, passed, tok_out, 1 + 4 * i + t + 1)
                        zt = z[0:rows, t % 2, :]
                        here = bass.ds(i * TB + t * P, rows)
                        kv = O["fox_kv_p"][here, :] if blk is not None else O["fox_kv_s"]
                        nkv = O["nsa_kv_p"][here, :] if blk is not None else O["nsa_kv_s"]
                        sp.dma_start(kv, zt[:, 0:512]).then_inc(tok_stored[t % 2], 16)
                        sp.dma_start(S["hgrn_v"][here, :], zt[:, 512:768]).then_inc(tok_stored[t % 2], 16)
                        sp.dma_start(nkv, zt[:, 768:1024]).then_inc(tok_stored[t % 2], 16)
                        sp.dma_start(S["win_kv"][here, :], zt[:, 1024:1152]).then_inc(tok_stored[t % 2], 16)
                    for n in range(5 * t, 5 * t + 5):
                        _, m, row, _ = FEAT[n]
                        hold(sp, passed, feat_out, 2 + NFEAT * i + n + 1)
                        sp.dma_start(S["feat"][row:row + m, bass.ds(i * TB, width)],
                                     fstage[0:m, n % 4, 0:width]).then_inc(feat_stored[n % 4], 16)
                hold(sp, passed, flog, 1 + 2 * i + 2)
                if blk is not None:
                    dst = O["fox_logf_p"][bass.ds(i * TB, TB), :].rearrange("(t p) h -> p t h", p=P)
                    sp.dma_start(dst, fl[:, 3, :].rearrange("p (t h) -> p t h", h=NH)).then_inc(flog_stored, 16)
                else:
                    sp.dma_start(O["fox_logf_s"], fl[0:TS, 3, 0:NH]).then_inc(flog_stored, 16)
            both(sp, store)
            for k in range(4):
                sp.wait_ge(feat_stored[k], 16 + 16 * 5 * (NBLK + 1))
            sp.wait_ge(tok_stored[0], 64 + 64 * (2 * NBLK + 1))
            sp.wait_ge(tok_stored[1], 64 + 64 * 2 * NBLK)
            sp.wait_ge(flog_stored, 16 + 16 * (NBLK + 1))
            sp.dma_start(O["nsa_win_p"], S["win_kv"][L - WIN:L, :]).then_inc(flog_stored, 16)
            sp.wait_ge(flog_stored, 32 + 16 * (NBLK + 1))

        @block.scalar
        def _(act):
            nc.scalar.preload_act_table_set(LN_EXP)
            for k in range(4):
                nc.scalar.sem_inc(feat_stored[k], 16)
            nc.scalar.sem_inc(feat_out, 2)

            def body(i, blk, rows, nt):
                width = TB if blk is not None else TS
                for t in range(nt):
                    act.wait_ge(x_loaded[t], 16 * (i + 1))
                    nc.scalar.activation(squares[0:rows, :], x[0:rows, t, :], ACT.Square,
                                         accum_out=ss[0:rows, t:t + 1]).then_inc(ss_done, 1)
                    act.wait_ge(ss_done, 4 * i + t + 1)
                    nc.scalar.activation(lnss[0:rows, t:t + 1], ss[0:rows, t:t + 1], ACT.Ln, scale=1.0 / D,
                                         bias=K["eps"][0:rows, :]).then_inc(ln_done, 1)
                    act.wait_ge(ln_done, 4 * i + t + 1)
                    nc.scalar.activation(rstd[0:rows, t:t + 1], lnss[0:rows, t:t + 1], ACT.Exp,
                                         scale=-0.5).then_inc(rstd_done, 1)
                for n in range(NFEAT):
                    _, m, _, scale = FEAT[n]
                    act.wait_ge(feat_mm, NFEAT * i + n + 1)
                    act.wait_ge(feat_stored[n % 4], 16 * (5 * i + n // 4 + 1))
                    nc.scalar.activation(fstage[0:m, n % 4, 0:width], p_feat[0:m, n % 2, 0:width], ACT.Copy,
                                         scale=scale).then_inc(feat_out, 1)
                n4 = nt * NH
                act.wait_ge(fabs_, i + 1)
                nc.scalar.activation(fl[0:rows, 2, 0:n4], fl[0:rows, 1, 0:n4], ACT.Exp, scale=-1.0).then_inc(fexp, 1)
                act.wait_ge(fexp, i + 1)
                nc.scalar.activation(fl[0:rows, 1, 0:n4], fl[0:rows, 2, 0:n4], ACT.Ln, bias=1.0).then_inc(fln, 1)
            both(act, body)

        @block.vector
        def _(dve):
            nc.vector.sem_inc(xn_done, 4)
            nc.vector.sem_inc(hT_done, 1)
            nc.vector.sem_inc(tok_out, 1)
            nc.vector.sem_inc(tok_stored[0], 64)
            nc.vector.sem_inc(tok_stored[1], 64)
            nc.vector.sem_inc(flog, 1)
            nc.vector.sem_inc(flog_stored, 16)
            dve.wait_ge(consts, 32)

            def body(i, blk, rows, nt):
                for t in range(nt):
                    dve.wait_ge(rstd_done, 4 * i + t + 1)
                    dve.wait_ge(turned, 4 * i + t + 1)
                    nc.vector.tensor_scalar(xn[0:rows, t, :], x[0:rows, t, :], rstd[0:rows, t:t + 1], None,
                                            ALU.mult).then_inc(xn_done, 1)
                for t in range(nt):
                    dve.wait_ge(turned, 4 + 4 * i + t + 1)
                    nc.vector.tensor_tensor(hT[:, :, t * P:t * P + rows],
                                            p_turn[:].rearrange("p (c q) -> p c q", c=KC)[:, :, 0:rows],
                                            bc(gain[:], 2, rows), ALU.mult).then_inc(hT_done, 1)
                for t in range(nt):
                    dve.wait_ge(tok_mm, 4 * i + t + 1)
                    if blk is not None:
                        dve.wait_ge(tok_stored[t % 2], 64 * (2 * i + t // 2 + 1))
                        dve.wait_ge(flog_stored, 16 * (i + 1))
                    else:
                        dve.wait_ge(tok_stored[0], 64 * (2 * NBLK + 1))
                        dve.wait_ge(flog_stored, 16 * (NBLK + 1))
                    zt = z[0:rows, t % 2, :]
                    nc.vector.tensor_copy(zt[:, 0:512], p_tok[0:rows, 0, :])
                    nc.vector.tensor_copy(zt[:, 512:768], p_tok[0:rows, 1, 0:256])
                    nc.vector.tensor_tensor(fl[0:rows, 0, t * NH:(t + 1) * NH], p_tok[0:rows, 1, 256:260],
                                            fbias[0:rows, :], ALU.add).then_inc(fz, 1)
                    nc.vector.tensor_copy(zt[:, 768:1152], p_tok[0:rows, 2, 0:384]).then_inc(tok_out, 1)
                n4 = nt * NH
                dve.wait_ge(fz, 4 * i + nt)
                nc.vector.scalar_tensor_tensor(out=fl[0:rows, 1, 0:n4], in0=fl[0:rows, 0, 0:n4], scalar=-1.0,
                                               in1=fl[0:rows, 0, 0:n4], op0=ALU.mult, op1=ALU.max).then_inc(fabs_, 1)
                nc.vector.tensor_single_scalar(fl[0:rows, 3, 0:n4], fl[0:rows, 0, 0:n4], 0.0,
                                               ALU.min).then_inc(flog, 1)
                dve.wait_ge(fln, i + 1)
                dve.wait_ge(flog, 1 + 2 * i + 1)
                nc.vector.tensor_tensor(fl[0:rows, 3, 0:n4], fl[0:rows, 3, 0:n4], fl[0:rows, 1, 0:n4],
                                        ALU.subtract).then_inc(flog, 1)
            both(dve, body)

        @block.tensor
        def _(pe):
            nc.tensor.sem_inc(turned, 4)

            def body(i, blk, rows, nt):
                width = TB if blk is not None else TS
                for t in range(nt):
                    pe.wait_ge(xn_done, 4 + 4 * i + t + 1)
                    pe.wait_ge(hT_done, 4 * i + t + 1)
                    for c in range(KC):
                        last = nc.tensor.transpose(p_turn[:, c * P:c * P + rows], xn[0:rows, t, c * P:(c + 1) * P],
                                                   K["ident"][0:rows, 0:rows])
                    last.then_inc(turned, 1)
                pe.wait_ge(hT_done, 1 + 4 * i + nt)
                for t in range(TILES):
                    if t < nt:
                        pe.wait_ge(tok_out, 4 * i + t + 1)
                        for dst, c0, m in ((p_tok[0:rows, 0, :], C_FK, 512), (p_tok[0:rows, 1, 0:256], C_HI, 256),
                                           (p_tok[0:rows, 1, 256:260], C_FF, 4), (p_tok[0:rows, 2, 0:384], C_NKV, 384)):
                            if t == 0:
                                pe.wait_ge(w_loaded[w_group(c0)], 16)
                            for c in range(KC):
                                last = nc.tensor.matmul(dst, hT[:, c, t * P:t * P + rows], w[:, c, c0:c0 + m],
                                                        start=(c == 0), stop=(c == KC - 1))
                        last.then_inc(tok_mm, 1)
                    for n in range(5 * t, 5 * t + 5):
                        c0, m, _, _ = FEAT[n]
                        pe.wait_ge(feat_out, NFEAT * i + n + 1)
                        if c0 is None:
                            pe.wait_ge(small_loaded, 32)
                        else:
                            pe.wait_ge(w_loaded[w_group(c0)], 16)
                        for c in range(KC):
                            lhsT = w_small[:, c, :] if c0 is None else w[:, c, c0:c0 + m]
                            last = nc.tensor.matmul(p_feat[0:m, n % 2, 0:width], lhsT, hT[:, c, 0:width],
                                                    start=(c == 0), stop=(c == KC - 1))
                        last.then_inc(feat_mm, 1)
            both(pe, body)


class Steps:

    def __init__(self, engine, sem, i=0, per=0):
        self.engine, self.sem, self.start, self.per, self.n = engine, sem, i * per, per, 0

    def __call__(self, instruction):
        self.n += 1
        instruction.then_inc(self.sem, 1)
        self.engine.wait_ge(self.sem, self.start + self.n)

    def closed(self, instruction, passed):
        self(instruction)
        self.engine.sem_inc(passed, 1)

    def end(self):
        assert self.per == self.n, (self.per, self.n)


F32R = mybir.dt.float32r


def split(v, step, x, high, low):
    step(v.tensor_copy(high, x))
    step(v.tensor_tensor(low, x, high.bitcast(F32), ALU.subtract))


def stage_gates(nc, I, O, S, K):
    with Room(nc, "gates") as r:
        z = r.sb("z", [16, T])
        a = r.sb("a", [16, T])
        e = r.sb("e", [16, T])
        ls = r.sb("ls", [16, T])
        g = r.sb("g", [16, T])
        one = r.sb("one", [4, L])
        negsum = r.sb("negsum", [4, L])
        bias = r.sb("bias", [16, 1])
        loaded, absd, expd, lnd, lsd, stored = (r.sem(n) for n in ("loaded", "abs", "exp", "ln", "logsig", "stored"))
        zero, summed, gated, biased = (r.sem(n) for n in ("zero", "summed", "gated", "biased"))
        block = r.block()

        @block.sync
        def _(sp):
            sp.dma_start(z[:], S["feat"][R_SM:R_SM + 16, :]).then_inc(loaded, 16)
            sp.wait_ge(zero, 1)
            sp.dma_start(bias[0:NH, :], I["b_fox_f"].unsqueeze(1)).then_inc(loaded, 16)
            sp.wait_ge(summed, 1)
            sp.dma_start(S["keyc"], negsum[:]).then_inc(stored, 16)
            sp.wait_ge(gated, 1)
            sp.dma_start(S["gates"], g[:]).then_inc(stored, 16)
            sp.wait_ge(stored, 32)

        @block.vector
        def _(dve):
            nc.vector.memset(bias[:], 0.0).then_inc(zero, 1)
            nc.vector.memset(one[:], 1.0).then_inc(zero, 1)
            dve.wait_ge(loaded, 32)
            nc.vector.tensor_scalar(z[:], z[:], bias[:, 0:1], None, ALU.add).then_inc(biased, 1)
            dve.wait_ge(biased, 1)
            nc.vector.scalar_tensor_tensor(out=a[:], in0=z[:], scalar=-1.0, in1=z[:], op0=ALU.mult,
                                           op1=ALU.max).then_inc(absd, 1)
            dve.wait_ge(lnd, 1)
            nc.vector.scalar_tensor_tensor(out=ls[:], in0=z[:], scalar=0.0, in1=a[:], op0=ALU.min,
                                           op1=ALU.subtract).then_inc(lsd, 1)
            dve.wait_ge(lsd, 1)
            dve.wait_ge(zero, 2)
            nc.vector.tensor_tensor_scan(negsum[:], one[:], ls[0:4, 0:L], 0.0, ALU.mult,
                                         ALU.subtract).then_inc(summed, 1)

        @block.scalar
        def _(act):
            nc.scalar.preload_act_table_set(LN_EXP)
            act.wait_ge(absd, 1)
            nc.scalar.activation(e[:], a[:], ACT.Exp, scale=-1.0).then_inc(expd, 1)
            act.wait_ge(expd, 1)
            nc.scalar.activation(a[:], e[:], ACT.Ln, bias=1.0).then_inc(lnd, 1)
            act.wait_ge(lsd, 1)
            nc.scalar.activation(g[:], ls[:], ACT.Exp).then_inc(gated, 1)


NCMP = L // 32
NSEL = L // 64


def top16(v, step, passed, imp, best, work, off, bias_out):
    step.closed(v.max(best, imp), passed)
    step.closed(v.match_replace(work, best, imp, -3e38), passed)
    step.closed(v.max(best, work), passed)
    step(v.match_replace(work, best, work, -3e38))
    step(v.tensor_single_scalar(off, work, -1e38, ALU.is_gt))
    step(v.scalar_tensor_tensor(out=work, in0=imp, scalar=0.0, in1=off, op0=ALU.is_lt, op1=ALU.max))
    step.closed(v.tensor_single_scalar(bias_out, work, NEG, ALU.mult), passed)


def stage_select(nc, I, O, S, K):
    PAIR = 2
    PASSES = L // P // PAIR
    with Room(nc, "sel") as r:
        cmp = r.sb("cmp", [P, L])
        w_rows = r.sb("w_rows", [32, P])
        wT = r.sb("wT", [P, 32])
        kvT = r.sb("kvT", [P, NCMP])
        vc = r.sb("vc", [NCMP, P])
        valid = r.sb("valid", [P, L // P, NCMP])
        vbias = r.sb("vbias", [P, L // P, NCMP])
        keep = r.sb("keep", [P, L // P, NSEL])
        force = r.sb("force", [P, L // P, NSEL])
        q = r.sb("q", [HD, PAIR, NH, P])
        s = r.sb("s", [P, PAIR, NH, NCMP])
        e = r.sb("e", [P, PAIR, NH, NCMP])
        m = r.sb("m", [P, PAIR * NH])
        d = r.sb("d", [P, PAIR * NH])
        imp = r.sb("imp", [P, PAIR, NSEL])
        best = r.sb("best", [P, PAIR, 8])
        work = r.sb("work", [P, PAIR, NSEL])
        off = r.sb("off", [P, PAIR, NSEL])
        sbias = r.sb("sbias", [P, PAIR, NSEL])
        pT = r.sb("pT", [HD, PAIR, NH * P])
        bT = r.sb("bT", [NSEL, PAIR * P])
        oT = r.sb("oT", [HD, PAIR, NH * P])
        p_s = r.ps("p_s", [P, PAIR, 512])
        p_t = r.ps("p_t", [P, PAIR, 512])
        p_b = r.ps("p_b", [P, 512])
        p_o = r.ps("p_o", [P, PAIR, 512])
        passed_dve, passed_pe = r.sem("passed_dve"), r.sem("passed_pe")
        ready, w_turned, prepared, masks, steps = (r.sem(n) for n in ("ready", "w_turned", "prepared", "masks", "steps"))
        q_loaded, scored, shifted, expd, probs, turned, copied, o_done, o_out, stored = (
            r.sem(n) for n in ("q_loaded", "scored", "shifted", "exp", "probs", "turned", "copied", "o_done", "o_out",
                               "stored"))
        block = r.block()

        @block.gpsimd
        def _(pool):
            nc.gpsimd.memset(valid[:], 1.0)
            nc.gpsimd.memset(keep[:], 1.0)
            nc.gpsimd.memset(force[:], 0.0).then_inc(masks, 1)
            pool.wait_ge(masks, 1)
            nc.gpsimd.affine_select(out=valid[:], in_=valid[:], pattern=[[P, L // P], [-32, NCMP]], base=-31,
                                    channel_multiplier=1, compare_op=ALU.is_ge, fill=0.0)
            nc.gpsimd.affine_select(out=keep[:], in_=keep[:], pattern=[[P, L // P], [-64, NSEL]], base=-64,
                                    channel_multiplier=1, compare_op=ALU.is_ge, fill=0.0)
            nc.gpsimd.affine_select(out=force[:], in_=force[:], pattern=[[P, L // P], [-64, NSEL]], base=-64,
                                    channel_multiplier=1, compare_op=ALU.is_ge, fill=1e9).then_inc(masks, 1)
            pool.wait_ge(masks, 2)
            nc.gpsimd.memset(keep[:, :, 0:1], 0.0)
            nc.gpsimd.affine_select(out=force[:], in_=force[:], pattern=[[P, L // P], [-64, NSEL]], base=0,
                                    channel_multiplier=1, compare_op=ALU.is_ge, fill=-1e9).then_inc(masks, 1)
            pool.wait_ge(masks, 3)
            nc.gpsimd.memset(force[:, :, 0:1], 1e9).then_inc(masks, 1)

        @block.sync
        def _(sp):
            sp.dma_start(cmp[:], S["feat"][R_CMP:R_CMP + P, 0:L]).then_inc(ready, 16)
            for kv in range(2):
                sp.dma_start(w_rows[:, kv * HD:(kv + 1) * HD], I["nsa_cmp_w"][kv]).then_inc(ready, 16)
            sp.sem_inc(stored, 48)
            nq = S["feat"][R_NQ:R_NQ + GW, :].rearrange("(h d) t -> d h t", h=NH)
            oc = S["group"][G_CMP:G_CMP + GW, :].rearrange("(h d) t -> d h t", h=NH)
            passed = r.sem("passed")
            with sp.Fori(0, PASSES) as i:
                hold(sp, passed, scored, i + 1)
                for u in range(PAIR):
                    sp.dma_start(q[:, u, :, :], nq[:, :, bass.ds(i * (PAIR * P) + u * P, P)]).then_inc(q_loaded, 16)
                hold(sp, passed, copied, 2 * i + 1)
                sp.dma_start(S["sel_bias"][:, bass.ds(i * (PAIR * P), PAIR * P)], bT[:]).then_inc(stored, 16)
                hold(sp, passed, o_out, i + 1)
                for u in range(PAIR):
                    sp.dma_start(oc[:, :, bass.ds(i * (PAIR * P) + u * P, P)],
                                 oT[:, u, :].rearrange("d (h t) -> d h t", h=NH)).then_inc(stored, 16)
            sp.wait_ge(stored, 48 * (PASSES + 1))

        @block.tensor
        def _(pe):
            pe.wait_ge(ready, 48)
            nc.tensor.transpose(p_t[:, 0, 0:32], w_rows[:], K["ident"][0:32, 0:32]).then_inc(w_turned, 1)
            pe.wait_ge(prepared, 1)
            nc.tensor.transpose(p_t[0:NCMP, 1, 0:P], kvT[:], K["ident"][:]).then_inc(w_turned, 1)
            pe.wait_ge(prepared, 2)
            pe.sem_inc(scored, 1)
            with pe.Fori(0, PASSES) as i:
                pe.wait_ge(q_loaded, 32 * i + 32)
                for u in range(PAIR):
                    for h in range(NH):
                        last = nc.tensor.matmul(p_s[:, u, h * NCMP:(h + 1) * NCMP], q[:, u, h, :], kvT[0:HD, :],
                                                start=True, stop=True)
                last.then_inc(scored, 1)
                pe.wait_ge(probs, i + 1)
                for u in range(PAIR):
                    nc.tensor.transpose(p_b[0:NSEL, u * P:(u + 1) * P], sbias[:, u, :], K["ident"][:])
                    for h in range(NH):
                        last = nc.tensor.transpose(p_t[0:NCMP, u, h * P:(h + 1) * P], e[:, u, h, :], K["ident"][:])
                last.then_inc(turned, 1)
                hold(pe, passed_pe, copied, 2 * i + 2)
                for u in range(PAIR):
                    last = nc.tensor.matmul(p_o[0:HD, u, :], vc[:, HD:P], pT[:, u, :], start=True, stop=True)
                last.then_inc(o_done, 1)

        @block.scalar
        def _(act):
            nc.scalar.preload_act_table_set(LN_EXP)
            with act.Fori(0, PASSES) as i:
                act.wait_ge(shifted, i + 1)
                nc.scalar.activation(e[:], s[:], ACT.Exp).then_inc(expd, 1)

        @block.vector
        def _(dve):
            v = nc.vector
            step = Steps(dve, steps)
            dve.wait_ge(w_turned, 1)
            step(v.tensor_copy(wT[:], p_t[:, 0, 0:32]))
            dve.wait_ge(ready, 48)
            blocks = cmp[:].rearrange("p (n j) -> p n j", j=32)
            step(v.tensor_tensor(blocks, blocks, bc(wT[:], 1, NCMP), ALU.mult))
            v.tensor_reduce(kvT[:], blocks, AX.X, ALU.add).then_inc(prepared, 1)
            dve.wait_ge(masks, 4)
            step(v.tensor_scalar(vbias[:], valid[:], -NEG, NEG, ALU.mult, ALU.add))
            dve.wait_ge(w_turned, 2)
            v.tensor_copy(vc[:], p_t[0:NCMP, 1, 0:P]).then_inc(prepared, 1)
            nsteps = 10 + 7 * PAIR
            first = 3
            with dve.Fori(0, PASSES) as i:
                step = Steps(dve, steps, i, nsteps)
                step.start = step.start + first
                pair = bass.ds(i * PAIR, PAIR)
                dve.wait_ge(scored, i + 2)
                step(v.tensor_tensor(s[:], p_s[:, :, 0:NH * NCMP].rearrange("p u (h n) -> p u h n", h=NH),
                                     bc(vbias[:, pair, :], 2, NH), ALU.add))
                rows = s[:].rearrange("p u h n -> p (u h) n")
                erows = e[:].rearrange("p u h n -> p (u h) n")
                step(v.tensor_reduce(m[:], rows, AX.X, ALU.max))
                v.tensor_tensor(rows, rows, bc(m[:], 2, NCMP), ALU.subtract).then_inc(shifted, 1)
                dve.wait_ge(expd, i + 1)
                step(v.tensor_tensor(e[:], e[:], bc(valid[:, pair, :], 2, NH), ALU.mult))
                step(v.tensor_reduce(d[:], erows, AX.X, ALU.add))
                step(v.tensor_single_scalar(d[:], d[:], 1.0, ALU.max))
                step(v.reciprocal(d[:], d[:]))
                step(v.tensor_tensor(erows, erows, bc(d[:], 2, NCMP), ALU.mult))
                for u in range(PAIR):
                    last = v.tensor_reduce(imp[:, u, :], e[:, u, :, :].rearrange("p h (b r) -> p b h r", r=2), AX.XY,
                                           ALU.add)
                step(last)
                step(v.tensor_tensor(imp[:], imp[:], keep[:, pair, :], ALU.mult))
                step.closed(v.tensor_tensor(imp[:], imp[:], force[:, pair, :], ALU.add), passed_dve)
                for u in range(PAIR):
                    top16(v, step, passed_dve, imp[:, u, :], best[:, u, :], work[:, u, :], off[:, u, :], sbias[:, u, :])
                v.sem_inc(probs, 1)
                dve.wait_ge(turned, i + 1)
                dve.wait_ge(stored, 48 * i + 48)
                v.tensor_copy(bT[:], p_b[0:NSEL, 0:PAIR * P]).then_inc(copied, 1)
                v.tensor_copy(pT[:], p_t[0:NCMP, :, :]).then_inc(copied, 1)
                dve.wait_ge(o_done, i + 1)
                v.tensor_copy(oT[:], p_o[0:HD, :, :]).then_inc(o_out, 1)
                step.end()


def plan_scores(window):
    steps = []
    for j in range(NBLK):
        tiles = []
        if window and j:
            tiles += [(4 * j - 4 + k, 0, P * (k + 1), P * k, "low_kq") for k in (3, 2, 1, 0)]
        elif not window:
            tiles += [(kt, 0, TB, None, None) for kt in range(4 * j)]
        tiles += [(4 * j + k, P * k, TB, P * k, "tri_kq") for k in range(4)]
        for n, t in enumerate(tiles):
            steps.append((j, *t, n == 0, n == len(tiles) - 1))
    return steps


def plan_maxima(window):
    pieces = []
    for i in range(L // P):
        k0 = max(0, i - 4) * P if window else 0
        end = (i + 1) * P
        for k in range(k0, end, 1024):
            n = min(1024, end - k)
            masks = [(n - P, "tri_qk")] if k + n == end else []
            if window and i >= 4:
                masks.append((0, "low_qk"))
            pieces.append((i, k, n, (k - k0) // 1024, masks))
    return pieces


def stage_attend(nc, I, O, S, K, kind):
    window = kind == "win"
    steps, pieces = plan_scores(window), plan_maxima(window)
    NS, NP_ = len(steps), len(pieces)
    assert NS % 4 == 0 and NP_ % 2 == 0
    r_q = R_FQ if kind == "fox" else R_NQ
    g_out = {"fox": G_FOX, "sel": G_SEL, "win": G_WIN}[kind]
    with Room(nc, "att_" + kind) as r:
        q_raw, k_raw = r.sb("q_raw", [P, L]), r.sb("k_raw", [P, L])
        q, k = r.sb("q", [P, 2, L], F32R), r.sb("k", [P, 2, L], F32R)
        ql, kl = r.sb("ql", [P, 2, L], F32R), r.sb("kl", [P, 2, L], F32R)
        v1 = r.sb("v1", [P, 2, L // P, P])
        e = r.sb("e", [P, 4, TB])
        mx = r.sb("mx", [P, 2, L // P])
        m = r.sb("m", [P, L // P])
        mp = r.sb("mp", [P, L // P, 33])
        lnd = r.sb("lnd", [HD, 2, TB])
        rec = r.sb("rec", [HD, 2, TB])
        o = r.sb("o", [HD, 2, TB])
        p_m = r.ps("p_m", [P, 2, 1024])
        p_s = r.ps("p_s", [P, 2, TB])
        p_o = r.ps("p_o", [P, 2, TB])
        ones_set, rows_set, loaded = r.sem("ones_set"), r.sem("rows_set"), r.pool_sem("loaded")
        passed, passed_pool = r.sem("passed"), r.sem("passed_pool")
        pieced, reduced, m_ready, m_turned, m_rows = (r.sem(n) for n in ("pieced", "reduced", "m_ready", "m_turned", "m_rows"))
        scored, expd, pv, head_done = (r.sem(n) for n in ("scored", "exp", "pv", "head_done"))
        lnd_done, rec_done, o_out, stored = r.sem("lnd_done"), r.sem("rec_done"), r.sem("o_out"), r.sems("stored", 2)
        v_loaded = r.pool_sems("v_loaded", 2)
        qk_split, qk_steps, low_set, m_steps, m_low_row = (r.sem(n) for n in ("qk_split", "qk_steps", "low_set", "m_steps", "m_low_row"))
        nload = 3 if kind == "fox" else 2
        block = r.block()
        NSET = {"fox": 3, "sel": 2, "win": 2}[kind]

        @block.gpsimd
        def _(pool):
            nc.gpsimd.memset(v1[:, :, :, HD:P], 1.0).then_inc(ones_set, 1)
            if kind == "sel":
                made = r.sem("made")
                pool.wait_ge(ones_set, 1)
                nc.gpsimd.memset(k_raw[HD:96, :], 1.0).then_inc(made, 1)
                pool.wait_ge(made, 1)
                nc.gpsimd.affine_select(out=k_raw[HD:96, :], in_=k_raw[HD:96, :], pattern=[[1, L]], base=0,
                                        channel_multiplier=-64, compare_op=ALU.is_ge, fill=0.0).then_inc(made, 1)
                pool.wait_ge(made, 2)
                nc.gpsimd.affine_select(out=k_raw[HD:96, :], in_=k_raw[HD:96, :], pattern=[[-1, L]], base=63,
                                        channel_multiplier=64, compare_op=ALU.is_ge, fill=0.0).then_inc(rows_set, 1)

            if kind == "sel":
                pool.dma_start(q_raw[HD:96, :], S["sel_bias"]).then_inc(loaded, 16)

            def load(head, u):
                hold(pool, passed_pool, qk_split, head + 1)
                if kind == "fox":
                    krow, vsrc = bass.ds(head * HD + R_FK, HD), O["fox_kv_p"][:, bass.ds(head * HD + GW, HD)]
                elif kind == "sel":
                    krow, vsrc = slice(R_KS, R_KS + HD), O["nsa_kv_p"][:, 3 * HD:4 * HD]
                else:
                    krow, vsrc = slice(R_KW, R_KW + HD), S["win_kv"][0:L, HD:2 * HD]
                pool.dma_start(q_raw[0:HD, :], S["feat"][bass.ds(head * HD + r_q, HD), 0:L]).then_inc(loaded, 16)
                pool.dma_start(k_raw[0:HD, :], S["feat"][krow, 0:L]).then_inc(loaded, 16)
                if kind == "fox":
                    pool.wait_ge(rows_set, NSET)
                    pool.dma_start(k_raw[HD:HD + 1, :], S["keyc"][bass.ds(head, 1), :]).then_inc(loaded, 16)
                hold(pool, passed_pool, head_done, head + 1)
                pool.dma_start(v1[:, u, :, 0:HD], vsrc.rearrange("(k p) d -> p k d", p=P)).then_inc(v_loaded[u], 16)

            with pool.Fori(0, NH // 2) as i:
                for u in range(2):
                    load(2 * i + u, u)

        @block.sync
        def _(sp):
            sp.sem_inc(stored[0], 16)
            sp.sem_inc(stored[1], 16)

            def store(head):
                for j in range(NBLK):
                    hold(sp, passed, o_out, 2 + NBLK * head + j + 1)
                    sp.dma_start(S["group"][bass.ds(head * HD + g_out, HD), j * TB:(j + 1) * TB],
                                 o[:, j % 2, :]).then_inc(stored[j % 2], 16)

            with sp.Fori(0, NH // 2) as i:
                for u in range(2):
                    store(2 * i + u)
            for u in range(2):
                sp.wait_ge(stored[u], 16 + 16 * 2 * NH)

        once = 16 if kind == "sel" else 0

        @block.tensor
        def _(pe):
            pe.wait_ge(ones_set, 1)
            pe.wait_ge(rows_set, NSET)
            pe.sem_inc(head_done, 2)
            pe.sem_inc(pv, 4)

            def body(head, u, i):
                pe.wait_ge(qk_split, 1 + head + 1)
                for n, (t, k0, width, _, masks) in enumerate(pieces):
                    pe.wait_ge(reduced, NP_ * head + n + 1)
                    dst = p_m[:, n % 2, :]
                    for c in range(0, width, TB):
                        w = min(TB, width - c)
                        here = [(a, name) for a, name in masks if c <= a < c + w]
                        for a, b in ((ql, k), (q, kl), (q, k)):
                            last = nc.tensor.matmul(dst[:, c:c + w], a[0:96, u, t * P:(t + 1) * P],
                                                    b[0:96, u, k0 + c:k0 + c + w], start=a is ql,
                                                    stop=a is q and b is k and not here)
                        for a, name in here:
                            last = nc.tensor.matmul(dst[:, a:a + P], K["ident"][:], K[name][:], start=False,
                                                    stop=(a, name) == here[-1])
                    last.then_inc(pieced, 1)
                pe.wait_ge(m_ready, head + 1)
                for t in range(L // P):
                    last = nc.tensor.matmul(p_m[0:33, t // 8, (t % 8) * P:(t % 8 + 1) * P], mp[:, t, :],
                                            K["ident"][:], start=True, stop=True)
                last.then_inc(m_turned, 1)
                pe.wait_ge(v_loaded[u], 16 * i + 16)
                pe.wait_ge(m_rows, head + 1)
                pe.wait_ge(m_low_row, head + 1)
                LAG = 2
                for n in range(NS + LAG):
                    if n < NS:
                        j, kt, x0, x1, mcol, mask, first, _ = steps[n]
                        pe.wait_ge(expd, NS * head + n + 1)
                        for a, b in ((kl, q), (k, ql), (k, q)):
                            last = nc.tensor.matmul(p_s[:, n % 2, x0:x1], a[0:97, u, kt * P:(kt + 1) * P],
                                                    b[0:97, u, j * TB + x0:j * TB + x1], start=a is kl,
                                                    stop=a is k and b is q and mask is None)
                        if mask is not None:
                            last = nc.tensor.matmul(p_s[:, n % 2, mcol:mcol + P], K["ident"][:], K[mask][:],
                                                    start=False, stop=True)
                        last.then_inc(scored, 1)
                    if n >= LAG:
                        j, kt, x0, x1, _, _, first, final = steps[n - LAG]
                        if first:
                            pe.wait_ge(o_out, NBLK * head + j + 1)
                        pe.wait_ge(expd, 2 + NS * head + n - LAG + 1)
                        nc.tensor.matmul(p_o[:, j % 2, x0:x1], v1[:, u, kt, :], e[:, (n - LAG) % 4, x0:x1],
                                         start=first, stop=final).then_inc(pv, 1)
                pe.wait_ge(pv, 4 + NS * head + NS)
                pe.sem_inc(head_done, 1)

            with pe.Fori(0, NH // 2) as i:
                for u in range(2):
                    body(2 * i + u, u, i)

        @block.scalar
        def _(act):
            nc.scalar.preload_act_table_set(LN_EXP)
            act.sem_inc(expd, 2)

            def body(head, u):
                def reciprocal(j, n_last):
                    act.wait_ge(pv, 4 + NS * head + n_last + 1)
                    act.wait_ge(o_out, NBLK * head + j + 1)
                    nc.scalar.activation(lnd[:, j % 2, :], p_o[HD:P, j % 2, :], ACT.Ln).then_inc(lnd_done, 1)
                    act.wait_ge(lnd_done, NBLK * head + j + 1)
                    nc.scalar.activation(rec[:, j % 2, :], lnd[:, j % 2, :], ACT.Exp, scale=-1.0).then_inc(rec_done, 1)

                act.wait_ge(m_turned, head + 1)
                for b in range(2):
                    last = nc.scalar.activation(ql[96:97, u, b * 1024:(b + 1) * 1024], p_m[32:33, b, :],
                                                ACT.Copy, scale=-1.0)
                last.then_inc(m_low_row, 1)
                due = []
                for n, (j, kt, x0, x1, _, _, _, final) in enumerate(steps):
                    act.wait_ge(scored, NS * head + n + 1)
                    act.wait_ge(pv, NS * head + n + 1)
                    nc.scalar.activation(e[:, n % 4, x0:x1], p_s[:, n % 2, x0:x1], ACT.Exp).then_inc(expd, 1)
                    if final:
                        due.append((n + 3, j, n))
                    if due and due[0][0] == n:
                        _, jj, last = due.pop(0)
                        reciprocal(jj, last)
                for _, jj, last in due:
                    reciprocal(jj, last)

            with act.Fori(0, NH // 2) as i:
                for u in range(2):
                    body(2 * i + u, u)

        @block.vector
        def _(dve):
            v = nc.vector
            dve.sem_inc(reduced, 2)
            dve.sem_inc(o_out, 2)
            v.memset(mx[:], NEG)
            if kind == "fox":
                zeroed = r.sem("zeroed")
                v.memset(k_raw[HD:96, :], 0.0).then_inc(rows_set, 1)
                v.memset(q_raw[HD:96, :], 0.0).then_inc(zeroed, 1)
                dve.wait_ge(zeroed, 1)
                v.memset(q_raw[HD:HD + 1, :], 1.0).then_inc(rows_set, 1)
            elif kind == "win":
                v.memset(k_raw[HD:96, :], 0.0)
                v.memset(q_raw[HD:96, :], 0.0).then_inc(rows_set, 1)
            v.memset(k_raw[96:97, :], 1.0).then_inc(rows_set, 1)

            v.memset(mp[:], 0.0).then_inc(low_set, 1)
            dve.sem_inc(qk_split, 1)
            dve.wait_ge(rows_set, NSET)
            dve.wait_ge(low_set, 1)

            def split_head(step, u, head):
                dve.wait_ge(loaded, head * (16 * nload) + (once + 16 * nload))
                dve.wait_ge(head_done, head + 1)
                split(v, step, q_raw[0:96, :], q[0:96, u, :], ql[0:96, u, :])
                split(v, step, k_raw[0:97, :], k[0:97, u, :], kl[0:97, u, :])
                dve.sem_inc(qk_split, 1)

            def body(head, u, following):
                for n, (t, _, width, piece, _) in enumerate(pieces):
                    dve.wait_ge(pieced, NP_ * head + n + 1)
                    v.tensor_reduce(mx[:, piece, t:t + 1], p_m[:, n % 2, 0:width], AX.X, ALU.max).then_inc(reduced, 1)
                dve.wait_ge(reduced, 2 + NP_ * head + NP_)
                step = Steps(dve, m_steps, head, 2)
                step(v.tensor_tensor(m[:], mx[:, 0, :], mx[:, 1, :], ALU.max))
                step(v.tensor_copy(mp[:, :, 0].bitcast(F32R), m[:]))
                v.tensor_tensor(mp[:, :, 32], m[:], mp[:, :, 0], ALU.subtract).then_inc(m_ready, 1)
                dve.wait_ge(m_turned, head + 1)
                for b in range(2):
                    last = v.tensor_single_scalar(q[96:97, u, b * 1024:(b + 1) * 1024], p_m[0:1, b, :],
                                                  -1.0, ALU.mult)
                last.then_inc(m_rows, 1)
                if following:
                    split_head(*following)
                for j in range(NBLK):
                    dve.wait_ge(rec_done, NBLK * head + j + 1)
                    dve.wait_ge(stored[j % 2], 16 * (2 * head + j // 2 + 1))
                    v.tensor_tensor(o[:, j % 2, :], p_o[0:HD, j % 2, :], rec[:, j % 2, :], ALU.mult).then_inc(o_out, 1)

            split_head(Steps(dve, qk_steps), 0, 0)
            with dve.Fori(0, NH // 2 - 1) as i:
                for u in range(2):
                    step = Steps(dve, qk_steps, 2 * i + (u + 1), 4)
                    body(2 * i + u, u, (step, 1 - u, 2 * i + (u + 1)))
            body(NH - 2, 0, (Steps(dve, qk_steps, NH - 1, 4), 1, NH - 1))
            body(NH - 1, 1, None)


def stage_fox(nc, I, O, S, K):
    stage_attend(nc, I, O, S, K, "fox")


def stage_sel(nc, I, O, S, K):
    stage_attend(nc, I, O, S, K, "sel")


def stage_win(nc, I, O, S, K):
    stage_attend(nc, I, O, S, K, "win")


LEVELS = (64, 32, 16, 8, 4, 2, 1)


def lower_bounds(nc, step, low, lb):
    v = nc.vector
    return [
        lambda: step(v.tensor_tensor(lb["shift"][:], low[:], low[:], ALU.subtract)),
        lambda: step(v.reciprocal(lb["inv"][:], lb["exp"][:])),
        lambda: step(v.tensor_tensor(lb["soft"][:], lb["exp"][:], lb["inv"][:], ALU.mult)),
        lambda: step(v.tensor_tensor(lb["lb"][:], lb["soft"][:], lb["soft"][:], ALU.subtract)),
        lambda: step(v.tensor_scalar(lb["one_minus"][:], lb["lb"][:], -1.0, 1.0, ALU.mult, ALU.add)),
        lambda: step(v.tensor_single_scalar(lb["floored"][:], lb["lb"][:], 1e-30, ALU.max)),
    ]


LN2_60 = 60 * 0.6931471805599453


def hgrn_gates(nc, act, dve, r, z, a, b, tmp, raw_loaded, ncol):
    low = r.sb("low", [P, 2])
    gain = r.sb("gain", [P, 2])
    lb = {n: r.sb("lb_" + n, [P, 2]) for n in ("shift", "exp", "inv", "soft", "lb", "one_minus", "floored", "ln_om",
                                               "ln_lb")}
    vs, as_, handed, back = r.sem("gate_steps_dve"), r.sem("gate_steps_act"), r.sem("gates_to_act"), r.sem("gates_to_dve")
    v, s = nc.vector, nc.scalar

    def vector():
        step = Steps(dve, vs)
        todo = lower_bounds(nc, step, low, lb)
        dve.wait_ge(raw_loaded[0], raw_loaded[1])
        todo[0]()
        dve.sem_inc(handed, 1)
        dve.wait_ge(back, 1)
        for f in todo[1:]:
            f()
        step(v.scalar_tensor_tensor(out=a[:], in0=z[:], scalar=-1.0, in1=z[:], op0=ALU.mult, op1=ALU.max))
        dve.sem_inc(handed, 1)
        dve.wait_ge(back, 2)
        step(v.tensor_scalar(lb["ln_lb"][:], lb["ln_lb"][:], LN2_60, None, ALU.subtract))
        step(v.scalar_tensor_tensor(out=a[:], in0=z[:], scalar=0.0, in1=a[:], op0=ALU.min, op1=ALU.subtract))
        for c in range(2):
            step(v.tensor_scalar(b[:, c, 0:ncol], a[:, 1, c, :], lb["ln_om"][:, c:c + 1], None, ALU.add))
        step(v.tensor_tensor(a[:, 1], a[:, 1], z[:, 1], ALU.subtract))
        for c in range(2):
            step(v.tensor_scalar(tmp[:, c, :], b[:, c, 0:ncol], lb["ln_lb"][:, c:c + 1], None, ALU.subtract))
        dve.sem_inc(handed, 1)
        dve.wait_ge(back, 3)
        for c in range(2):
            step(v.scalar_tensor_tensor(out=b[:, c, 0:ncol], in0=b[:, c, 0:ncol], scalar=lb["ln_lb"][:, c:c + 1],
                                        in1=tmp[:, c, :], op0=ALU.max, op1=ALU.add))
        dve.wait_ge(back, 4)
        for n in (0, 2):
            step(v.tensor_tensor(z[:, n], z[:, n], a[:, n], ALU.mult))
        for c in range(2):
            step(v.tensor_scalar(z[:, 1, c, :], a[:, 1, c, :], lb["one_minus"][:, c:c + 1], None, ALU.mult))
            step(v.tensor_scalar(z[:, 2, c, :], z[:, 2, c, :], gain[:, c:c + 1], None, ALU.mult))
        return step

    def scalar():
        step = Steps(act, as_)
        act.wait_ge(handed, 1)
        step(s.activation(lb["exp"][:], lb["shift"][:], ACT.Exp))
        act.sem_inc(back, 1)
        act.wait_ge(handed, 2)
        step(s.activation(a[:], a[:], ACT.Exp, scale=-1.0))
        step(s.activation(a[:], a[:], ACT.Ln, bias=1.0))
        step(s.activation(lb["ln_om"][:], lb["one_minus"][:], ACT.Ln))
        step(s.activation(lb["ln_lb"][:], lb["floored"][:], ACT.Ln, scale=float(2 ** 60)))
        act.sem_inc(back, 1)
        act.wait_ge(handed, 3)
        step(s.activation(tmp[:], tmp[:], ACT.Abs))
        step(s.activation(tmp[:], tmp[:], ACT.Exp, scale=-1.0))
        step(s.activation(tmp[:], tmp[:], ACT.Ln, bias=1.0))
        act.sem_inc(back, 1)
        step(s.activation(a[:], a[:], ACT.Exp))
        act.sem_inc(back, 1)
        return step

    return low, gain, vector, scalar


def stage_hgrn(nc, I, O, S, K):
    NCH = L // P
    NL = len(LEVELS)
    with Room(nc, "hgrn") as r:
        z = r.sb("z", [P, 3, 2, L])
        a = r.sb("a", [P, 3, 2, L])
        b = r.sb("b", [P, 2, L + P])
        eb = r.sb("eb", [P, 2, L])
        ex = a[:].rearrange("p a b c -> p (a b c)")[:, 0:2 * 2048].rearrange("p (u l c t) -> p u l c t", u=2, l=8, c=2)
        qe = a[:].rearrange("p a b c -> p (a b c)")[:, 4096:8192].rearrange("p (u l c t) -> p u l c t", u=2, l=8, c=2)
        ke = r.sb("ke", [P, 2, 8, 2, P])
        am = a[:].rearrange("p a b c -> p (a b c)")[:, 8192:8192 + 2048].rearrange("p (u l t) -> p u l t", u=2, l=8)
        sq = a[:].rearrange("p a b c -> p (a b c)")[:, 0:2 * L].rearrange("p (c t) -> p c t", c=2)
        o = r.sb("o", [P, 2, L])
        v = r.sb("v", [P, 2, GW])
        kdT = r.sb("kdT", [P, 2 * P])
        qb = r.sb("qb", [P, 2, 2, P])
        st = r.sb("st", [P, 2, HD])
        once = r.sb("once", [P, L])
        mask = r.sb("mask", [P, 8, P])
        p_a = r.ps("p_a", [P, 2, 1024])
        p_t = r.ps("p_t", [P, 512])
        p_u = r.ps("p_u", [P, 512])
        p_o = r.ps("p_o", [P, 2, 512])
        loaded, masks, v_loaded = r.sem("loaded"), r.sem("masks"), r.pool_sems("v_loaded", 2)
        scanned, diffed, exd, factors, kd_turned, kd_out = (r.sem(n) for n in ("scanned", "diffed", "exd", "factors",
                                                                              "kd_turned", "kd_out"))
        absd, paired, masked, updated, o_done, o_out, v_used = (r.sem(n) for n in (
            "absd", "paired", "masked", "updated", "o_done", "o_out", "v_used"))
        su, ebd, stored, sqd, summed, rsd, normed, lnd = (r.sem(n) for n in ("su", "ebd", "stored", "sqd", "summed", "rsd",
                                                                      "normed", "lnd"))
        low, gain, gates_dve, gates_act = hgrn_gates(nc, nc.scalar, nc.vector, r, z, a, b, eb, (loaded, 16 * 8), L)
        block = r.block()

        @block.sync
        def _(sp):
            for n, row in enumerate((R_HQ, R_HF, R_HG)):
                for c in range(2):
                    sp.dma_start(z[:, n, c, :], S["feat"][row + c * P:row + (c + 1) * P, 0:L]).then_inc(loaded, 16)
            sp.dma_start(low[:], I["hgrn_lower"].rearrange("(c p) -> p c", p=P),
                         allow_slow_non_contiguous=True).then_inc(loaded, 16)
            sp.dma_start(gain[:], I["g_mix"][GW:2 * GW].rearrange("(c p) -> p c", p=P),
                         allow_slow_non_contiguous=True).then_inc(loaded, 16)
            sp.wait_ge(normed, 2)
            for c in range(2):
                sp.dma_start(S["group"][G_HGRN + c * P:G_HGRN + (c + 1) * P, 0:L], o[:, c, :]).then_inc(stored, 16)
                sp.dma_start(O["hgrn_p"][2 * c:2 * c + 2].rearrange("h k v -> (h k) v"), st[:, c, :]).then_inc(stored, 16)
            sp.wait_ge(stored, 64)

        @block.gpsimd
        def _(pool):
            step = Steps(pool, masks)
            step(nc.gpsimd.memset(mask[:], 1.0))
            for l, m in enumerate(LEVELS):
                n = P // (2 * m)
                view = mask[:, l, :].rearrange("p (n w) -> p n w", w=2 * m)
                for pattern, base, mult in (([[0, n], [1, 2 * m]], -m, 0), ([[-2 * m, n], [0, 2 * m]], 0, 1),
                                            ([[2 * m, n], [0, 2 * m]], m - 1, -1)):
                    step(nc.gpsimd.affine_select(out=view, in_=view, pattern=pattern, base=base,
                                                 channel_multiplier=mult, compare_op=ALU.is_ge, fill=0.0))
            step(nc.gpsimd.affine_select(out=mask[:, NL, :], in_=mask[:, NL, :], pattern=[[-1, P]], base=0,
                                         channel_multiplier=1, compare_op=ALU.is_equal, fill=0.0))
            nmask = step.n
            assert nmask == 23
            passed = r.sem("passed")
            with pool.Fori(0, NCH // 2) as i:
                for u in range(2):
                    hold(pool, passed, v_used, 2 * i + u + 1)
                    pool.dma_start(v[:, u, :], S["hgrn_v"][bass.ds(i * 2 * P + u * P, P), :]).then_inc(v_loaded[u], 16)

        @block.scalar
        def _(act):
            nc.scalar.preload_act_table_set(LN_EXP)
            gates_act()
            s = nc.scalar
            act.wait_ge(scanned, 1)
            s.activation(eb[:], b[:, :, 0:L], ACT.Exp).then_inc(ebd, 1)

            def decays(j, u):
                act.wait_ge(diffed, j + 1)
                s.activation(ex[:, u], ex[:, u], ACT.Abs).then_inc(absd, 1)
                act.wait_ge(absd, j + 1)
                s.activation(ex[:, u], ex[:, u], ACT.Exp, scale=-1.0).then_inc(exd, 1)

            decays(0, 0)
            with act.Fori(0, NCH // 2) as i:
                for u in range(2):
                    j = 2 * i + u
                    act.wait_ge(kd_turned, j + 1)
                    s.activation(kdT[:], p_t[:, 0:2 * P], ACT.Copy).then_inc(kd_out, 1)
                    decays(j + 1, 1 - u)
                    act.wait_ge(o_done, j + 1)
                    s.activation(o[:, :, bass.ds(j * P, P)], p_o[:, u, 0:2 * P].rearrange("p (c t) -> p c t", c=2),
                                 ACT.Copy).then_inc(o_out, 1)
            act.wait_ge(o_out, 2 + NCH)
            act.wait_ge(masked, 4 * NCH + 2)
            act.wait_ge(su, 1 + NCH)
            s.activation(sq[:], o[:], ACT.Square).then_inc(sqd, 1)
            for n in range(2):
                act.wait_ge(summed, n + 1)
                for c in range(2):
                    s.activation(eb[:, n, c * 1024:(c + 1) * 1024], p_a[:, c, :], ACT.Ln, scale=1.0 / HD,
                                 bias=K["eps"][:]).then_inc(lnd, 1)
            act.wait_ge(lnd, 4)
            s.activation(eb[:], eb[:], ACT.Exp, scale=-0.5).then_inc(rsd, 1)

        @block.vector
        def _(dve):
            w = nc.vector
            dve.sem_inc(masked, 2)
            dve.sem_inc(v_used, 2)
            dve.sem_inc(o_out, 2)
            step = gates_dve()
            w.memset(b[:, :, L:L + P], 0.0)
            w.memset(st[:], 0.0)
            w.memset(once[:].rearrange("p (n t) -> p n t", t=P)[:, :, 1:P], 1.0)
            step(w.memset(once[:].rearrange("p (n t) -> p n t", t=P)[:, :, 0:1], 0.0))
            for c in range(2):
                step(w.tensor_tensor_scan(b[:, c, 0:L], once[:], b[:, c, 0:L], 0.0, ALU.mult, ALU.add))
            dve.sem_inc(scanned, 1)
            dve.wait_ge(ebd, 1)
            dve.wait_ge(masks, 23)

            def differences(j, u):
                bj = b[:, :, bass.ds(j * P, P)] if not isinstance(j, int) else b[:, :, j * P:(j + 1) * P]
                for l, m in enumerate(LEVELS):
                    n = P // (2 * m)
                    bv = bj.rearrange("p c (n w) -> p c n w", w=2 * m)
                    w.tensor_tensor(ex[:, u, l].rearrange("p c (n w) -> p c n w", w=2 * m), bv,
                                    bv[:, :, :, m - 1:m].broadcast_to([P, 2, n, 2 * m]), ALU.subtract)
                w.tensor_tensor(ex[:, u, NL], bj, bj[:, :, P - 1:P].broadcast_to([P, 2, P]),
                                ALU.subtract).then_inc(diffed, 1)

            def factor(j, u):
                at = bass.ds(j * P, P)
                qj, kj = z[:, 0, :, at], z[:, 1, :, at]
                dve.wait_ge(exd, j + 1)
                w.tensor_tensor(qb[:, u], qj, eb[:, :, at], ALU.mult)
                w.tensor_tensor(qe[:, u, 0:NL], ex[:, u, 0:NL], bc(qj, 1, NL), ALU.mult)
                w.tensor_copy(qe[:, u, NL], qj)
                w.tensor_tensor(ke[:, u, 0:NL], ex[:, u, 0:NL], bc(kj, 1, NL), ALU.mult)
                w.tensor_tensor(ex[:, u, NL], ex[:, u, NL], kj, ALU.mult)
                w.tensor_copy(ke[:, u, NL], kj).then_inc(factors, 1)

            def mask_pair(j, n):
                dve.wait_ge(paired, 4 * j + n + 1)
                dve.wait_ge(masked, 4 * j + n + 1)
                w.tensor_tensor(am[:, n % 2], p_a[:, n % 2, :].rearrange("p (l t) -> p l t", l=8), mask[:],
                                ALU.mult).then_inc(masked, 1)

            def chunk(j, u, last_chunk):
                mask_pair(j, 0)
                mask_pair(j, 1)
                if not last_chunk:
                    factor(j + 1, 1 - u)
                mask_pair(j, 2)
                mask_pair(j, 3)
                if not last_chunk:
                    dve.wait_ge(factors, j + 2)
                    differences(j + 2, u)
                dve.wait_ge(updated, 4 * j + 8)
                for c in range(2):
                    last = w.scalar_tensor_tensor(out=st[:, c, :], in0=st[:, c, :],
                                                  scalar=eb[:, c, bass.ds(j * P + P - 1, 1)],
                                                  in1=p_u[:, c * HD:(c + 1) * HD], op0=ALU.mult, op1=ALU.add)
                last.then_inc(su, 1)

            differences(0, 0)
            differences(1, 1)
            factor(0, 0)
            with dve.Fori(0, NCH // 2 - 1) as i:
                for u in range(2):
                    chunk(2 * i + u, u, False)
            chunk(NCH - 2, 0, False)
            chunk(NCH - 1, 1, True)
            dve.wait_ge(rsd, 1)
            dve.wait_ge(summed, 2)
            step(w.tensor_tensor(o[:], o[:], eb[:], ALU.mult))
            for c in range(2):
                w.tensor_tensor(o[:, c, :], o[:, c, :], z[:, 2, c, :], ALU.mult).then_inc(normed, 1)

        @block.tensor
        def _(pe):
            mm = nc.tensor.matmul
            r_passed = r.sem("passed_pe")
            pe.sem_inc(updated, 4)
            pe.sem_inc(su, 1)
            with pe.Fori(0, NCH // 2) as i:
                for u in range(2):
                    j = 2 * i + u
                    pe.wait_ge(factors, j + 1)
                    for c in range(2):
                        last = nc.tensor.transpose(p_t[:, c * P:(c + 1) * P], ex[:, u, NL, c, :], K["ident"][:])
                    last.then_inc(kd_turned, 1)
                    pe.wait_ge(v_loaded[u], 16 * i + 16)

                    def pair(n):
                        c, h = n // 2, HD * (n % 2)
                        pe.wait_ge(masked, 4 * j + n + 1)
                        for l in range(8):
                            last = mm(p_a[:, n % 2, l * P:(l + 1) * P], ke[h:h + HD, u, l, c, :], qe[h:h + HD, u, l, c, :],
                                      start=True, stop=True)
                        last.then_inc(paired, 1)

                    def weigh(n):
                        c, h = n // 2, HD * (n % 2)
                        pe.wait_ge(masked, 4 * j + n + 3)
                        dst = p_o[h:h + HD, u, c * P:(c + 1) * P]
                        for l in range(8):
                            mm(dst, v[:, u, n * HD:(n + 1) * HD], am[:, n % 2, l, :], start=(l == 0), stop=False)
                        return mm(dst, st[h:h + HD, c, :], qb[h:h + HD, u, c, :], start=False, stop=True)

                    pe.wait_ge(o_out, j + 1)
                    pe.wait_ge(su, j + 1)
                    pair(0)
                    pair(1)
                    for n in range(4):
                        last = weigh(n)
                        if n + 2 < 4:
                            pair(n + 2)
                    last.then_inc(o_done, 1)
                    hold(pe, r_passed, kd_out, j + 1)
                    for n in range(4):
                        c, h = n // 2, HD * (n % 2)
                        mm(p_u[h:h + HD, c * HD:(c + 1) * HD], kdT[:, n * HD:(n + 1) * HD],
                           v[:, u, n * HD:(n + 1) * HD], start=True, stop=True).then_inc(updated, 1)
                    pe.wait_ge(updated, 4 * j + 8)
                    pe.sem_inc(v_used, 1)
            pe.wait_ge(sqd, 1)
            for n in range(2):
                if n:
                    pe.wait_ge(lnd, 2)
                for c in range(4):
                    last = mm(p_a[:, c // 2, (c % 2) * 512:(c % 2 + 1) * 512], K["pairones"][:],
                              sq[:, n, c * 512:(c + 1) * 512], start=True, stop=True)
                last.then_inc(summed, 1)



def stage_lru(nc, I, O, S, K):
    NCOL = 416
    NLOAD = 2 * (3 + NB + 2) + 4
    with Room(nc, "lru") as r:
        xp = r.sb("xp", [P, 2, 3 + L])
        xs = r.sb("xs", [P, 2, NB, 3 + NT])
        gate = r.sb("gate", [P, 2, T])
        u = r.sb("u", [P, 2, T])
        a = r.sb("a", [P, 2, T])
        inp = r.sb("inp", [P, 2, T])
        th = r.sb("th", [P, 2, T])
        h = r.sb("h", [P, 2, T])
        wa = r.sb("wa", [P, 2, 2, P])
        cw = r.sb("cw", [P, 2, 4])
        col = {n: r.sb("col_" + n, [P, 2]) for n in ("cb", "ba", "bx", "lam", "abs", "exp", "ln", "rate", "nrate")}
        h0 = r.sb("h0", [P, 2, NB])
        p_g = r.ps("p_g", [P, 4, 512])
        loaded, zero, w_loaded, zeroed = (r.sem(n) for n in ("loaded", "zero", "w_loaded", "zeroed"))
        mixed, gated, gate_out, vs, as_, to_act, to_dve, done, stored = (
            r.sem(n) for n in ("mixed", "gated", "gate_out", "steps_dve", "steps_act", "to_act", "to_dve", "done",
                               "stored"))
        block = r.block()

        @block.sync
        def _(sp):
            n = 0
            for c in range(2):
                rows = slice(R_UX + c * P, R_UX + (c + 1) * P)
                sp.dma_start(xp[:, c, 3:3 + L], S["feat"][rows, 0:L]).then_inc(loaded, 16)
                sp.dma_start(xs[:, c, :, 3:], S["feat"][rows, L:T].rearrange("p (b t) -> p b t", t=NT)).then_inc(loaded, 16)
                sp.dma_start(gate[:, c, :], S["feat"][R_UG + c * P:R_UG + (c + 1) * P, :]).then_inc(loaded, 16)
                n += 3
                for b in range(NB):
                    sp.dma_start(xs[:, c, b, 0:3], I["state_lru_conv"][b, :, c * P:(c + 1) * P].rearrange("j p -> p j"),
                                 allow_slow_non_contiguous=True).then_inc(loaded, 16)
                    n += 1
                sp.dma_start(h0[:, c, :], I["state_lru_h"][:, c * P:(c + 1) * P].rearrange("b p -> p b"),
                             allow_slow_non_contiguous=True).then_inc(loaded, 16)
                sp.dma_start(cw[:, c, :], I["lru_conv_w"][:, c * P:(c + 1) * P].rearrange("j p -> p j"),
                             allow_slow_non_contiguous=True).then_inc(loaded, 16)
                n += 2
            for name, key in (("lru_conv_b", "cb"), ("lru_ba", "ba"), ("lru_bx", "bx"), ("lru_lambda", "lam")):
                sp.dma_start(col[key][:], I[name].rearrange("(c p) -> p c", p=P),
                             allow_slow_non_contiguous=True).then_inc(loaded, 16)
                n += 1
            assert n == NLOAD
            sp.wait_ge(zeroed, 1)
            for g, name in enumerate(("lru_wa", "lru_wx")):
                for k in range(4):
                    half = HD * (k % 2)
                    sp.dma_start(wa[half:half + HD, g, k // 2, half:half + HD], I[name][k]).then_inc(w_loaded, 16)
            sp.wait_ge(done, 1)
            for c in range(2):
                f = slice(c * P, (c + 1) * P)
                sp.dma_start(O["lru_h_p"][f].unsqueeze(1), h[:, c, L - 1:L]).then_inc(stored, 16)
                sp.dma_start(O["lru_h_s"][:, f].rearrange("b p -> p b"),
                             h[:, c, L:T].rearrange("p (b t) -> p b t", t=NT)[:, :, NT - 1],
                             allow_slow_non_contiguous=True).then_inc(stored, 16)
                sp.dma_start(O["lru_conv_p"][:, f].rearrange("j p -> p j"), xp[:, c, L:L + 3],
                             allow_slow_non_contiguous=True).then_inc(stored, 16)
                for b in range(NB):
                    sp.dma_start(O["lru_conv_s"][b, :, f].rearrange("j p -> p j"), xs[:, c, b, NT:NT + 3],
                                 allow_slow_non_contiguous=True).then_inc(stored, 16)
            sp.wait_ge(done, 2)
            for c in range(2):
                sp.dma_start(S["group"][G_LRU + c * P:G_LRU + (c + 1) * P, :], th[:, c, :]).then_inc(stored, 16)
            sp.wait_ge(stored, 16 * (2 * (3 + NB) + 2))

        @block.tensor
        def _(pe):
            pe.wait_ge(w_loaded, 128)
            pe.wait_ge(mixed, 1)
            n = 0
            for c in range(2):
                for k in range(T // NCOL):
                    for g in range(2):
                        if n >= 4:
                            pe.wait_ge(gate_out, n - 3)
                        nc.tensor.matmul(p_g[:, n % 4, 0:NCOL], wa[:, g, c, :], u[:, c, k * NCOL:(k + 1) * NCOL],
                                         start=True, stop=True).then_inc(gated, 1)
                        n += 1

        @block.scalar
        def _(act):
            s = nc.scalar
            step = Steps(act, as_)
            act.wait_ge(to_act, 1)
            step(s.activation(col["exp"][:], col["abs"][:], ACT.Exp, scale=-1.0))
            step(s.activation(col["ln"][:], col["exp"][:], ACT.Ln, bias=1.0))
            act.sem_inc(to_dve, 1)
            n = 0
            for c in range(2):
                for k in range(T // NCOL):
                    for dst, bias in ((a, "ba"), (inp, "bx")):
                        act.wait_ge(gated, n + 1)
                        s.activation(dst[:, c, k * NCOL:(k + 1) * NCOL], p_g[:, n % 4, 0:NCOL], ACT.Sigmoid,
                                     bias=col[bias][:, c:c + 1]).then_inc(gate_out, 1)
                        n += 1
            act.wait_ge(gate_out, n)
            act.wait_ge(to_act, 2)
            step(s.activation(h[:], h[:], ACT.Sigmoid, scale=1.5957691216057308))
            act.sem_inc(to_dve, 1)
            act.wait_ge(to_act, 3)
            for c in range(2):
                s.activation(th[:, c, :], a[:, c, :], ACT.Tanh, scale=col["nrate"][:, c:c + 1])
            for c in range(2):
                last = s.activation(a[:, c, :], a[:, c, :], ACT.Exp, scale=col["rate"][:, c:c + 1])
            step(last)
            act.sem_inc(to_dve, 1)
            act.wait_ge(to_act, 4)
            step(s.activation(th[:], th[:], ACT.Sqrt))
            act.sem_inc(to_dve, 1)

        @block.vector
        def _(dve):
            v = nc.vector
            step = Steps(dve, vs)
            v.memset(wa[:], 0.0).then_inc(zeroed, 1)
            step(v.memset(xp[:, :, 0:3], 0.0))
            dve.wait_ge(loaded, 16 * NLOAD)
            lam = col["lam"]
            step(v.scalar_tensor_tensor(out=col["abs"][:], in0=lam[:], scalar=-1.0, in1=lam[:], op0=ALU.mult,
                                        op1=ALU.max))
            dve.sem_inc(to_act, 1)
            xsv = [xs[:, c, :, :] for c in range(2)]
            for c in range(2):
                us = u[:, c, L:T].rearrange("p (b t) -> p b t", t=NT)
                for j in range(4):
                    w = cw[:, c, j:j + 1]
                    if j == 0:
                        v.tensor_scalar(u[:, c, 0:L], xp[:, c, 0:L], w, col["cb"][:, c:c + 1], ALU.mult, ALU.add)
                        step(v.tensor_scalar(us, xsv[c][:, :, 0:NT], w, col["cb"][:, c:c + 1], ALU.mult, ALU.add))
                    else:
                        v.scalar_tensor_tensor(out=u[:, c, 0:L], in0=xp[:, c, j:j + L], scalar=w, in1=u[:, c, 0:L],
                                               op0=ALU.mult, op1=ALU.add)
                        step(v.scalar_tensor_tensor(out=us, in0=xsv[c][:, :, j:j + NT], scalar=w, in1=us,
                                                    op0=ALU.mult, op1=ALU.add))
            dve.sem_inc(mixed, 1)
            dve.wait_ge(to_dve, 1)
            step(v.tensor_scalar(col["rate"][:], lam[:], -1.0, 0.0, ALU.mult, ALU.max))
            step(v.tensor_tensor(col["nrate"][:], col["rate"][:], col["ln"][:], ALU.add))
            step(v.tensor_scalar(col["rate"][:], col["nrate"][:], -8.0, None, ALU.mult))
            step(v.tensor_scalar(col["nrate"][:], col["rate"][:], -1.0, None, ALU.mult))
            step(v.tensor_tensor(h[:], gate[:], gate[:], ALU.mult))
            step(v.tensor_scalar(h[:], h[:], 0.044715, 1.0, ALU.mult, ALU.add))
            step(v.tensor_tensor(h[:], h[:], gate[:], ALU.mult))
            dve.sem_inc(to_act, 1)
            dve.wait_ge(to_dve, 2)
            step(v.tensor_tensor(gate[:], gate[:], h[:], ALU.mult))
            dve.wait_ge(gate_out, 4 * (T // NCOL))
            dve.sem_inc(to_act, 1)
            step(v.tensor_tensor(inp[:], inp[:], u[:], ALU.mult))
            dve.wait_ge(to_dve, 3)
            step(v.tensor_tensor(u[:], a[:], a[:], ALU.mult))
            step(v.scalar_tensor_tensor(out=th[:], in0=u[:], scalar=1.0, in1=th[:], op0=ALU.add, op1=ALU.mult))
            dve.sem_inc(to_act, 1)
            dve.wait_ge(to_dve, 4)
            step(v.tensor_tensor(inp[:], inp[:], th[:], ALU.mult))
            for c in range(2):
                first_a = a[:, c, L:T].rearrange("p (b t) -> p b t", t=NT)[:, :, 0]
                first_b = inp[:, c, L:T].rearrange("p (b t) -> p b t", t=NT)[:, :, 0]
                step(v.tensor_tensor(h0[:, c, :], h0[:, c, :], first_a, ALU.mult))
                step(v.tensor_tensor(first_b, first_b, h0[:, c, :], ALU.add))
                step(v.memset(first_a, 0.0))
                v.tensor_tensor_scan(h[:, c, 0:L], a[:, c, 0:L], inp[:, c, 0:L], 0.0, ALU.mult, ALU.add)
                step(v.tensor_tensor_scan(h[:, c, L:T], a[:, c, L:T], inp[:, c, L:T], 0.0, ALU.mult, ALU.add))
            dve.sem_inc(done, 1)
            step(v.tensor_tensor(th[:], h[:], gate[:], ALU.mult))
            dve.sem_inc(done, 1)


def stage_memory(nc, I, O, S, K):
    MT = MEM // P
    with Room(nc, "mem") as r:
        w = r.sb("w", [P, KC, 512])
        gain = r.sb("gain", [P, KC])
        x = r.sb("x", [P, MT, D])
        squares = r.sb("squares", [P, D])
        ss = r.sb("ss", [P, MT])
        hT = r.sb("hT", [P, KC, MEM])
        z = r.sb("z", [P, MT, 512])
        kT = r.sb("kT", [P, 2, MEM])
        p_turn = r.ps("p_turn", [P, MT, KC * P])
        p_z = r.ps("p_z", [P, MT, 512])
        p_k = r.ps("p_k", [P, 2, 512])
        loaded, sums, rstd, xn, turned, hT_done, mm, out, stored = (
            r.sem(n) for n in ("loaded", "sums", "rstd", "xn", "turned", "hT_done", "mm", "out", "stored"))
        block = r.block()

        @block.sync
        def _(sp):
            sp.dma_start(x[:], I["mem_prompt"].rearrange("(t p) d -> p t d", p=P)).then_inc(loaded, 16)
            sp.dma_start(gain[:], I["g_mem"].rearrange("(c p) -> p c", p=P), allow_slow_non_contiguous=True).then_inc(loaded, 16)
            sp.dma_start(w[:], I["xa_wkv"].rearrange("(c p) n -> p c n", p=P)).then_inc(loaded, 16)
            sp.wait_ge(out, 2)
            sp.dma_start(O["xa_kv_p"].rearrange("(t p) n -> p t n", p=P), z[:]).then_inc(stored, 16)
            sp.dma_start(S["xa_k"].rearrange("(c p) m -> p c m", p=P), kT[:]).then_inc(stored, 16)
            sp.wait_ge(stored, 32)

        @block.scalar
        def _(act):
            nc.scalar.preload_act_table_set(LN_EXP)
            step = Steps(act, rstd)
            act.wait_ge(loaded, 48)
            for t in range(MT):
                last = nc.scalar.activation(squares[:], x[:, t, :], ACT.Square, accum_out=ss[:, t:t + 1])
                step(last)
            step(nc.scalar.activation(ss[:], ss[:], ACT.Ln, scale=1.0 / D, bias=K["eps"][:]))
            step(nc.scalar.activation(ss[:], ss[:], ACT.Exp, scale=-0.5))

        @block.vector
        def _(dve):
            v = nc.vector
            dve.wait_ge(rstd, MT + 2)
            for t in range(MT):
                v.tensor_scalar(x[:, t, :], x[:, t, :], ss[:, t:t + 1], None, ALU.mult).then_inc(xn, 1)
            for t in range(MT):
                dve.wait_ge(turned, t + 1)
                v.tensor_tensor(hT[:, :, t * P:(t + 1) * P], p_turn[:, t, :].rearrange("p (c q) -> p c q", c=KC),
                                bc(gain[:], 2, P), ALU.mult).then_inc(hT_done, 1)
            dve.wait_ge(mm, 2)
            v.tensor_copy(z[:], p_z[:]).then_inc(out, 1)
            v.tensor_copy(kT[:], p_k[:, :, 0:MEM]).then_inc(out, 1)

        @block.tensor
        def _(pe):
            for t in range(MT):
                pe.wait_ge(xn, t + 1)
                for c in range(KC):
                    last = nc.tensor.transpose(p_turn[:, t, c * P:(c + 1) * P], x[:, t, c * P:(c + 1) * P], K["ident"][:])
                last.then_inc(turned, 1)
            pe.wait_ge(hT_done, MT)
            for t in range(MT):
                for c in range(KC):
                    last = nc.tensor.matmul(p_z[:, t, :], hT[:, c, t * P:(t + 1) * P], w[:, c, :], start=(c == 0),
                                            stop=(c == KC - 1))
            last.then_inc(mm, 1)
            for n in range(2):
                for c in range(KC):
                    last = nc.tensor.matmul(p_k[:, n, 0:MEM], w[:, c, n * P:(n + 1) * P], hT[:, c, :], start=(c == 0),
                                            stop=(c == KC - 1))
            last.then_inc(mm, 1)


def stage_residual(nc, I, O, S, K, tag, weight, n_in, source, residual, result, g_post, g_next, mix=False, wq=False,
                   keep_h=False):
    with Room(nc, tag) as r:
        w = r.sb("w", [P, n_in, D])
        gpost = r.sb("gpost", [P, D])
        gnext = r.sb("gnext", [P, KC])
        x = r.sb("x", [P, TILES, D])
        y = r.sb("y", [P, n_in, TB] if mix else [P, 2, n_in, P])
        tmp = r.sb("tmp", [P, D])
        squares = r.sb("squares", [P, D])
        ss = r.sb("ss", [P, TILES, 2])
        p_y = r.ps("p_y", [P, 2, D])
        per_load = max(1, n_in // 8)
        loaded, w_loaded, wq_loaded = r.sem("loaded"), r.sems("w_loaded", n_in // per_load), r.sem("wq_loaded")
        x_loaded, x_stored = r.pool_sems("x_loaded", TILES), r.sems("x_stored", TILES)
        y_loaded, y_mm, x_done = r.pool_sems("y_loaded", 2), r.sem("y_mm"), r.sem("x_done")
        posted, s_act = r.sem("posted"), r.sem("steps_act")
        rstd1, rstd2 = r.sem("rstd1"), r.sem("rstd2")
        NCONST = 1 + (g_next is not None) + mix
        NMLOAD = 3 + 3 + 4
        if g_next is not None:
            xn = r.sb("xn", [P, 2, D])
            hT = r.sb("hT", [P, KC, TB])
            p_turn = r.ps("turn", [P, KC * P])
            xn_done, turned, hT_done, h_stored = (r.sem(n) for n in ("xn_done", "turned", "hT_done", "h_stored"))
        if wq:
            wqs = r.sb("wq", [P, KC, GW])
            qT = r.sb("qT", [P, 2, TB])
            q_mm, q_out, q_stored = r.sem("q_mm"), r.sem("q_out"), r.sem("q_stored")
        if mix:
            gm = r.sb("gm", [P, KC])
            raw = r.sb("raw", [P, KC, TB])
            nsa = r.sb("nsa", [P, 3, 2, TB])
            gates = r.sb("gates", [P, 3, 2, TB])
            sq = r.sb("sq", [P, 3, 2, TB])
            rs = r.sb("rs", [P, 3, TB])
            combined, squared, summed, ln_g, rs_done, made, m_steps = (r.sem(n) for n in (
                "combined", "squared", "summed", "ln_g", "rs_done", "made", "m_steps"))
            m_loaded = r.pool_sem("m_loaded")
        if mix or wq:
            p_r = r.ps("p_r", [P, 2, TB])
        passed, passed_pool = r.sem("passed"), r.sem("passed_pool")
        block = r.block()

        def both(engine, body):
            with engine.Fori(0, NBLK - 1) as i:
                body(i, P, TILES, TB, (i + 1, TB))
            body(NBLK - 1, P, TILES, TB, (NBLK, TS))
            body(NBLK, TS, 1, TS, None)

        @block.gpsimd
        def _(pool):
            def load_groups(i, width):
                here = bass.ds(i * TB, width) if width == TB else slice(L, T)
                hold(pool, passed_pool, made, i + 1)
                for k, g in ((0, G_FOX), (2, G_HGRN), (6, G_LRU)):
                    pool.dma_start(raw[:, k:k + 2, 0:width],
                                   S["group"][g:g + GW, here].rearrange("(c p) t -> p c t", p=P)).then_inc(m_loaded, 16)
                for k, g in enumerate((G_CMP, G_SEL, G_WIN)):
                    pool.dma_start(nsa[:, k, :, 0:width],
                                   S["group"][g:g + GW, here].rearrange("(c p) t -> p c t", p=P)).then_inc(m_loaded, 16)
                for c in range(2):
                    for half in range(2):
                        row = 4 + 3 * (2 * c + half)
                        pool.dma_start(gates[half * HD:(half + 1) * HD, :, c, 0:width],
                                       bc(S["gates"][row:row + 3, here], 0, HD)).then_inc(m_loaded, 16)

            if mix:
                load_groups(0, TB)

            def loads(i, rows, nt, width, following):
                for t in range(nt):
                    tile = bass.ds(i * TB + t * P, P) if nt > 1 else slice(L, T)
                    if g_next is not None:
                        hold(pool, passed_pool, xn_done, 4 * i + t + 1)
                    hold(pool, passed_pool, x_stored[t], 16 * (i + 1))
                    src = residual(tile, nt > 1)
                    pool.dma_start(x[0:rows, t, :], src).then_inc(x_loaded[t], 16)
                    if not mix:
                        hold(pool, passed_pool, y_mm, 4 * i + t + 3)
                        pool.dma_start(y[:, t % 2, :, 0:rows],
                                       source[:, tile].rearrange("(c p) t -> p c t", p=P)).then_inc(y_loaded[t % 2], 16)
                if mix and following:
                    load_groups(*following)
            both(pool, loads)

        @block.sync
        def _(sp):
            for t in range(TILES):
                sp.sem_inc(x_stored[t], 16)
            sp.dma_start(gpost[:], I["norms"][g_post].partition_broadcast(P)).then_inc(loaded, 16)
            n = 1
            if g_next is not None:
                sp.dma_start(gnext[:], I["norms"][g_next].rearrange("(c p) -> p c", p=P),
                             allow_slow_non_contiguous=True).then_inc(loaded, 16)
                sp.sem_inc(h_stored, 16)
                n += 1
            if mix:
                sp.dma_start(gm[:], I["g_mix"].rearrange("(c p) -> p c", p=P), allow_slow_non_contiguous=True).then_inc(loaded, 16)
                n += 1
            assert n == NCONST, n
            if not mix:
                sp.wait_ge(y_loaded[0], 16)
            for k in range(n_in // per_load):
                cs = slice(k * per_load, (k + 1) * per_load)
                sp.dma_start(w[:, cs, :], I[weight][k * per_load * P:(k + 1) * per_load * P, :].rearrange(
                    "(c p) n -> p c n", p=P)).then_inc(w_loaded[k], 16)
            if wq:
                sp.dma_start(wqs[:], I["xa_wq"].rearrange("(c p) n -> p c n", p=P)).then_inc(wq_loaded, 16)
                sp.sem_inc(q_stored, 32)

            def stores(i, rows, nt, width, following):
                here = bass.ds(i * TB, width) if nt > 1 else slice(L, T)
                for t in range(nt):
                    hold(sp, passed, x_done, 4 * i + t + 1)
                    tile = bass.ds(i * TB + t * P, P) if nt > 1 else slice(L, T)
                    sp.dma_start(result(tile, nt > 1), x[0:rows, t, :]).then_inc(x_stored[t], 16)
                if keep_h:
                    hold(sp, passed, hT_done, 1 + 4 * i + nt)
                    sp.dma_start(S["h3"][:, here].rearrange("(c p) t -> p c t", p=P), hT[:, :, 0:width]).then_inc(h_stored, 16)
                if wq:
                    hold(sp, passed, q_out, 2 * i + 4)
                    for c in range(2):
                        sp.dma_start(S["xa_q"][c * P:(c + 1) * P, here], qT[:, c, 0:width]).then_inc(q_stored, 16)
            both(sp, stores)
            for t in range(TILES):
                sp.wait_ge(x_stored[t], 16 + 16 * (NBLK + (t == 0)))
            if keep_h:
                sp.wait_ge(h_stored, 16 + 16 * (NBLK + 1))
            if wq:
                sp.wait_ge(q_stored, 32 + 32 * (NBLK + 1))

        @block.scalar
        def _(act):
            nc.scalar.preload_act_table_set(LN_EXP)
            s = nc.scalar

            def norm(i, rows, src, t, k, sem):
                step = Steps(act, s_act)
                step.start = nsteps_before(i, t, k)
                step(s.activation(squares[0:rows, :], src, ACT.Square, accum_out=ss[0:rows, t, k:k + 1]))
                step(s.activation(ss[0:rows, t, k:k + 1], ss[0:rows, t, k:k + 1], ACT.Ln, scale=1.0 / D,
                                  bias=K["eps"][0:rows, :]))
                s.activation(ss[0:rows, t, k:k + 1], ss[0:rows, t, k:k + 1], ACT.Exp, scale=-0.5).then_inc(sem, 1)

            def nsteps_before(i, t, k):
                per_tile = 4 if g_next is not None else 2
                return per_tile * (TILES * i + t) + 2 * k

            def square_groups(i, width):
                act.wait_ge(combined, i + 1)
                s.activation(sq[:, 0, :, 0:width], raw[:, 0:2, 0:width], ACT.Square)
                s.activation(sq[:, 1, :, 0:width], raw[:, 4:6, 0:width], ACT.Square)
                s.activation(sq[:, 2, :, 0:width], raw[:, 6:8, 0:width], ACT.Square).then_inc(squared, 1)

            def scale_groups(i, width):
                act.wait_ge(made, i + 1)
                for g in range(3):
                    act.wait_ge(summed, 3 * i + g + 1)
                    s.activation(rs[:, g, 0:width], p_r[:, g % 2, 0:width], ACT.Ln, scale=1.0 / GW,
                                 bias=K["eps"][:]).then_inc(ln_g, 1)
                act.wait_ge(ln_g, 3 * i + 3)
                s.activation(rs[:, :, 0:width], rs[:, :, 0:width], ACT.Exp, scale=-0.5).then_inc(rs_done, 1)

            def body(i, rows, nt, width, following):
                for t in range(nt):
                    if mix and following and t == 2:
                        square_groups(*following)
                    act.wait_ge(y_mm, 4 + 4 * i + t + 1)
                    norm(i, rows, p_y[0:rows, t % 2, :], t, 0, rstd1)
                    if g_next is not None:
                        act.wait_ge(x_done, 4 * i + t + 1)
                        norm(i, rows, x[0:rows, t, :], t, 1, rstd2)
                if mix and following:
                    scale_groups(*following)
                if wq:
                    for c in range(2):
                        act.wait_ge(q_mm, 2 * i + c + 1)
                        act.wait_ge(q_stored, 32 * i + 32)
                        s.activation(qT[:, c, 0:width], p_r[:, c, 0:width], ACT.Copy, scale=QSCALE).then_inc(q_out, 1)
            if wq:
                act.sem_inc(q_out, 2)
            if mix:
                square_groups(0, TB)
                scale_groups(0, TB)
            both(act, body)

        @block.vector
        def _(dve):
            v = nc.vector
            dve.sem_inc(posted, 2)
            if mix:
                dve.sem_inc(made, 1)
            if g_next is not None:
                dve.sem_inc(hT_done, 1)
                dve.sem_inc(xn_done, 4)
            dve.wait_ge(loaded, 16 * NCONST)

            def combine(i, width):
                dve.wait_ge(m_loaded, 16 * NMLOAD * (i + 1))
                step = Steps(dve, m_steps, i, 2)
                step(v.tensor_tensor(nsa[:, :, :, 0:width], nsa[:, :, :, 0:width], gates[:, :, :, 0:width], ALU.mult))
                step(v.tensor_tensor(nsa[:, 0, :, 0:width], nsa[:, 0, :, 0:width], nsa[:, 1, :, 0:width], ALU.add))
                v.tensor_tensor(raw[:, 4:6, 0:width], nsa[:, 0, :, 0:width], nsa[:, 2, :, 0:width],
                                ALU.add).then_inc(combined, 1)

            def body(i, rows, nt, width, following):
                if mix:
                    dve.wait_ge(rs_done, i + 1)
                    dve.wait_ge(combined, i + 1)
                    dve.wait_ge(y_mm, 4 * i + 4)
                    v.tensor_copy(y[:, 2:4, 0:width], raw[:, 2:4, 0:width])
                    for g, k in ((0, 0), (1, 4), (2, 6)):
                        for c in (k, k + 1):
                            last = v.scalar_tensor_tensor(out=y[:, c, 0:width], in0=raw[:, c, 0:width],
                                                          scalar=gm[:, c:c + 1], in1=rs[:, g, 0:width],
                                                          op0=ALU.mult, op1=ALU.mult)
                    last.then_inc(made, 1)

                def post(t):
                    dve.wait_ge(x_done, 4 * i + t)
                    dve.wait_ge(rstd1, 4 * i + t + 1)
                    v.scalar_tensor_tensor(out=tmp[0:rows, :], in0=p_y[0:rows, t % 2, :], scalar=ss[0:rows, t, 0:1],
                                           in1=gpost[0:rows, :], op0=ALU.mult, op1=ALU.mult).then_inc(posted, 1)
                    dve.wait_ge(x_loaded[t], 16 * (i + 1))
                    dve.wait_ge(posted, 2 + 4 * i + t + 1)
                    v.tensor_tensor(x[0:rows, t, :], x[0:rows, t, :], tmp[0:rows, :], ALU.add).then_inc(x_done, 1)

                def normalise(t):
                    dve.wait_ge(rstd2, 4 * i + t + 1)
                    dve.wait_ge(turned, 2 + 4 * i + t + 1)
                    v.tensor_scalar(xn[0:rows, t % 2, :], x[0:rows, t, :], ss[0:rows, t, 1:2], None,
                                    ALU.mult).then_inc(xn_done, 1)

                def take(t):
                    dve.wait_ge(turned, 4 + 4 * i + t + 1)
                    if t == 0 and keep_h:
                        dve.wait_ge(h_stored, 16 * (i + 1))
                    v.tensor_tensor(hT[:, :, t * P:t * P + rows],
                                    p_turn[:].rearrange("p (c q) -> p c q", c=KC)[:, :, 0:rows],
                                    bc(gnext[:], 2, rows), ALU.mult).then_inc(hT_done, 1)

                for t in range(nt):
                    if t and g_next is not None:
                        normalise(t - 1)
                    post(t)
                    if t and g_next is not None:
                        take(t - 1)
                    if mix and following and t == 1:
                        combine(*following)
                if g_next is not None:
                    normalise(nt - 1)
                    take(nt - 1)
            if mix:
                combine(0, TB)
            both(dve, body)

        @block.tensor
        def _(pe):
            mm = nc.tensor.matmul
            pe.sem_inc(y_mm, 4)
            if g_next is not None:
                pe.sem_inc(turned, 4)

            def sum_groups(i, width, p_r_wait):
                pe.wait_ge(squared, i + 1)
                pe.wait_ge(q_out, p_r_wait)
                for g in range(3):
                    if g == 2:
                        pe.wait_ge(ln_g, 3 * i + 1)
                    for c in range(2):
                        last = mm(p_r[:, g % 2, 0:width], K["ones"][:], sq[:, g, c, 0:width], start=(c == 0),
                                  stop=(c == 1))
                    last.then_inc(summed, 1)

            if mix:
                sum_groups(0, TB, 2)

            def body(i, rows, nt, width, following):
                if mix:
                    pe.wait_ge(made, 1 + i + 1)

                def turn(t):
                    pe.wait_ge(xn_done, 4 + 4 * i + t + 1)
                    pe.wait_ge(hT_done, 4 * i + t + 1)
                    for c in range(KC):
                        last = nc.tensor.transpose(p_turn[:, c * P:c * P + rows], xn[0:rows, t % 2, c * P:(c + 1) * P],
                                                   K["ident"][0:rows, 0:rows])
                    last.then_inc(turned, 1)

                for t in range(nt):
                    if not mix:
                        per = (TILES // 2) * 16
                        pe.wait_ge(y_loaded[t % 2], per * i + 16 * (t // 2 + 1))
                    pe.wait_ge(posted, 4 * i + t + 1)
                    for c in range(n_in):
                        if t == 0 and c % per_load == 0:
                            pe.wait_ge(w_loaded[c // per_load], 16)
                        lhsT = y[:, c, t * P:t * P + rows] if mix else y[:, t % 2, c, 0:rows]
                        for n in range(2):
                            last = mm(p_y[0:rows, t % 2, n * 512:(n + 1) * 512], lhsT, w[:, c, n * 512:(n + 1) * 512],
                                      start=(c == 0), stop=(c == n_in - 1))
                    last.then_inc(y_mm, 1)
                    if t and g_next is not None:
                        turn(t - 1)
                if mix and following:
                    sum_groups(*following, 2 * i + 2)
                if g_next is not None:
                    turn(nt - 1)
                if wq:
                    pe.wait_ge(ln_g, 3 * i + (6 if following else 3))
                    pe.wait_ge(hT_done, 1 + 4 * i + nt)
                    pe.wait_ge(wq_loaded, 16)
                    for n in range(2):
                        for c in range(KC):
                            last = mm(p_r[:, n, 0:width], wqs[:, c, n * P:(n + 1) * P], hT[:, c, 0:width],
                                      start=(c == 0), stop=(c == KC - 1))
                        last.then_inc(q_mm, 1)
            both(pe, body)


def stage_cross(nc, I, O, S, K):
    MT = MEM // P
    ORDER = (0, 2, 1, 3)
    with Room(nc, "xa") as r:
        kT = r.sb("kT", [P, 2, MEM])
        v = r.sb("v", [P, MT, GW])
        q = r.sb("q", [P, 2, 2, TB])
        e = r.sb("e", [P, 2, NH, MEM])
        m = r.sb("m", [P, 2, NH])
        d = r.sb("d", [P, 2, NH])
        rd = r.sb("rd", [P, 2, NH])
        eT = r.sb("eT", [P, NH * MT, TB])
        o = r.sb("o", [P, 2, TB])
        p_s = r.ps("p_s", [P, 2, NH * MEM])
        p_t = r.ps("p_t", [P, 1024])
        p_o = r.ps("p_o", [P, 2, TB])
        loaded, q_loaded = r.sem("loaded"), r.pool_sems("q_loaded", 2)
        passed, passed_pool, passed_pe = r.sem("passed"), r.sem("passed_pool"), r.sem("passed_pe")
        scored, maxed, expd, summed, weighed, turned, copied, o_mm, o_out, stored = (
            r.sem(n) for n in ("scored", "maxed", "expd", "summed", "weighed", "turned", "copied", "o_mm", "o_out", "stored"))
        block = r.block()

        @block.gpsimd
        def _(pool):
            with pool.Fori(0, NBLK // 2) as i:
                for u in range(2):
                    hold(pool, passed_pool, o_mm, 2 * i + u + 1)
                    pool.dma_start(q[:, u, :, :], S["xa_q"][:, bass.ds(i * 2 * TB + u * TB, TB)].rearrange(
                        "(c p) t -> p c t", p=P)).then_inc(q_loaded[u], 16)

        @block.sync
        def _(sp):
            sp.dma_start(kT[:], S["xa_k"].rearrange("(c p) m -> p c m", p=P)).then_inc(loaded, 16)
            sp.dma_start(v[:], O["xa_kv_p"][:, GW:2 * GW].rearrange("(t p) n -> p t n", p=P)).then_inc(loaded, 16)
            sp.sem_inc(stored, 16)
            with sp.Fori(0, NBLK) as i:
                hold(sp, passed, o_out, i + 1)
                sp.dma_start(S["xa_o"][:, bass.ds(i * TB, TB)].rearrange("(c p) t -> p c t", p=P), o[:]).then_inc(stored, 16)
            sp.wait_ge(stored, 16 * (NBLK + 1))

        @block.tensor
        def _(pe):
            mm = nc.tensor.matmul
            pe.sem_inc(o_mm, 2)
            pe.wait_ge(loaded, 32)
            with pe.Fori(0, NBLK // 2) as i:
                for u in range(2):
                    blk = 2 * i + u
                    pe.wait_ge(q_loaded[u], 16 * i + 16)

                    def score(t):
                        n = 4 * blk + t
                        pe.wait_ge(weighed, n + 1)
                        for n, h in enumerate(ORDER):
                            half = HD * (h % 2)
                            last = mm(p_s[:, t % 2, n * MEM:(n + 1) * MEM],
                                      q[half:half + HD, u, h // 2, t * P:(t + 1) * P], kT[half:half + HD, h // 2, :],
                                      start=True, stop=True)
                        last.then_inc(scored, 1)

                    def turn(t):
                        n = 4 * blk + t
                        pe.wait_ge(weighed, 2 + n + 1)
                        pe.wait_ge(copied, n + 1)
                        for h in range(NH):
                            for c in range(MT):
                                last = nc.tensor.transpose(p_t[:, (h * MT + c) * P:(h * MT + c + 1) * P],
                                                           e[:, t % 2, h, c * P:(c + 1) * P], K["ident"][:])
                        last.then_inc(turned, 1)

                    score(0)
                    for t in range(TILES):
                        if t + 1 < TILES:
                            score(t + 1)
                        turn(t)
                    hold(pe, passed_pe, copied, 1 + 4 * blk + 4)
                    for n, h in enumerate(ORDER):
                        half = HD * (h % 2)
                        for c in range(MT):
                            last = mm(p_o[half:half + HD, h // 2, :], v[:, c, h * HD:(h + 1) * HD], eT[:, n * MT + c, :],
                                      start=(c == 0), stop=(c == MT - 1))
                    last.then_inc(o_mm, 1)

        @block.scalar
        def _(act):
            nc.scalar.preload_act_table_set(LN_EXP)
            s = nc.scalar
            act.sem_inc(copied, 1)
            with act.Fori(0, NBLK) as i:
                for t in range(TILES):
                    n = 4 * i + t
                    act.wait_ge(maxed, n + 1)
                    for h in range(NH):
                        last = s.activation(e[:, t % 2, h, :], p_s[:, t % 2, h * MEM:(h + 1) * MEM], ACT.Exp,
                                            bias=m[:, t % 2, h:h + 1], accum_out=d[:, t % 2, h:h + 1])
                    last.then_inc(expd, 1)
                    if t:
                        act.wait_ge(turned, n)
                        act.wait_ge(o_mm, 2 + i)
                        s.activation(eT[:, :, (t - 1) * P:t * P], p_t[:].rearrange("p (a q) -> p a q", q=P),
                                     ACT.Copy).then_inc(copied, 1)
                act.wait_ge(turned, 4 * i + 4)
                s.activation(eT[:, :, 3 * P:4 * P], p_t[:].rearrange("p (a q) -> p a q", q=P), ACT.Copy).then_inc(copied, 1)

        @block.vector
        def _(dve):
            w = nc.vector
            dve.sem_inc(weighed, 2)
            with dve.Fori(0, NBLK) as i:
                for t in range(TILES):
                    n = 4 * i + t
                    dve.wait_ge(scored, n + 1)
                    w.tensor_reduce(rd[:, t % 2, :], p_s[:, t % 2, :].rearrange("p (h m) -> p h m", h=NH), AX.X,
                                    ALU.max).then_inc(summed, 1)
                    dve.wait_ge(summed, 2 * n + 1)
                    w.tensor_single_scalar(m[:, t % 2, :], rd[:, t % 2, :], -1.0, ALU.mult).then_inc(maxed, 1)
                    dve.wait_ge(expd, n + 1)
                    w.reciprocal(rd[:, t % 2, :], d[:, t % 2, :]).then_inc(summed, 1)
                    dve.wait_ge(summed, 2 * n + 2)
                    w.tensor_tensor(e[:, t % 2], e[:, t % 2], bc(rd[:, t % 2, :], 2, MEM), ALU.mult).then_inc(weighed, 1)
                dve.wait_ge(o_mm, 2 + i + 1)
                dve.wait_ge(stored, 16 * i + 16)
                w.tensor_copy(o[:], p_o[:]).then_inc(o_out, 1)


def stage_ff1(nc, I, O, S, K):
    QUARTERS = 4
    NF, GRP, WGRP = FF // P // QUARTERS, 2, 2
    NG, NW = NF // GRP, NF // WGRP
    NB5 = NBLK + 1
    with Room(nc, "ff1") as r:
        w_raw = r.sb("w_raw", [P, NW, KC, WGRP * P])
        w = r.sb("w", [P, KC, NF * P], F32R)
        wl = r.sb("wl", [P, KC, NF * P], F32R)
        h_raw = r.sb("h_raw", [P, KC, TB])
        h = r.sb("h", [P, 2, KC, TB], F32R)
        hl = r.sb("hl", [P, 2, KC, TB], F32R)
        hs = r.sb("hs", [P, 2, KC, TS], F32R)
        f = r.sb("f", [P, 2, GRP, TB])
        p_f = r.ps("p_f", [P, 4, TB])
        w_loaded, h_loaded = r.sems("w_loaded", NW), r.pool_sem("h_loaded")
        w_split, h_split = r.sem("w_split"), r.sem("h_split")
        passed, passed_pool, passed_pe, steps, rectified = (
            r.sem(n) for n in ("passed", "passed_pool", "passed_pe", "steps", "rectified"))
        f_mm, f_out, f_stored = r.sem("f_mm"), r.sem("f_out"), r.sems("f_stored", 2)
        block = r.block()

        blocks = [(k % 2, slice(k * TB, (k + 1) * TB), TB) for k in range(NBLK)]
        blocks.append((2, slice(L, T), TS))

        def parts(slot):
            return (hs[:, 0], hs[:, 1]) if slot == 2 else (h[:, slot], hl[:, slot])

        @block.gpsimd
        def _(pool):
            with pool.Fori(0, QUARTERS) as quarter:
                for k, (_, tokens, width) in enumerate(blocks):
                    hold(pool, passed_pool, h_split, quarter * NB5 + k + 1)
                    pool.dma_start(h_raw[:, :, 0:width], S["h3"][:, tokens].rearrange("(c p) t -> p c t", p=P)
                                   ).then_inc(h_loaded, 16)

        @block.sync
        def _(sp):
            for u in range(2):
                sp.sem_inc(f_stored[u], 16)
            sp.wait_ge(h_loaded, 16)

            with sp.Fori(0, QUARTERS) as quarter:
                for g in range(NW):
                    hold(sp, passed, w_split, quarter * NW + g + 1)
                    cols = bass.ds(quarter * (NF * P) + g * WGRP * P, WGRP * P)
                    sp.dma_start(w_raw[:, g], I["w_ff1"][:, cols].rearrange("(c p) n -> p c n", p=P)).then_inc(w_loaded[g], 16)
                for k, (_, tokens, width) in enumerate(blocks):
                    for g in range(NG):
                        hold(sp, passed, f_out, quarter * (NB5 * NF) + 4 + NF * k + GRP * (g + 1))
                        rows = bass.ds(quarter * (NF * P) + g * GRP * P, GRP * P)
                        sp.dma_start(S["ff"][rows, tokens].rearrange("(c p) t -> p c t", p=P),
                                     f[:, g % 2, :, 0:width]).then_inc(f_stored[g % 2], 16)
            for u in range(2):
                sp.wait_ge(f_stored[u], 16 + 16 * (NG // 2) * NB5 * QUARTERS)

        @block.tensor
        def _(pe):
            pe.sem_inc(f_mm, 2 * NF)
            with pe.Fori(0, QUARTERS) as quarter:
                for k, (slot, _, width) in enumerate(blocks):
                    hold(pe, passed_pe, h_split, quarter * NB5 + k + 2)
                    hh, hlow = parts(slot)
                    for n in range(NF):
                        if k == 0 and n % WGRP == 0:
                            hold(pe, passed_pe, w_split, quarter * NW + (NW + n // WGRP + 1))
                        pe.wait_ge(f_out, quarter * (NB5 * NF) + NF * k + n + 1)
                        cols = slice(n * P, (n + 1) * P)
                        for c in range(KC):
                            for wp, hp in ((wl, hh), (w, hlow), (w, hh)):
                                last = nc.tensor.matmul(p_f[:, n % 4, 0:width], wp[:, c, cols],
                                                        hp[:, c, 0:width], start=(c == 0 and wp is wl),
                                                        stop=(c == KC - 1 and wp is w and hp is hh))
                        last.then_inc(f_mm, 1)
        @block.vector
        def _(dve):
            v = nc.vector
            dve.sem_inc(f_out, 4)
            dve.sem_inc(h_split, 1)
            dve.sem_inc(w_split, NW)
            with dve.Fori(0, QUARTERS) as quarter:
                step = Steps(dve, steps, quarter, 2 * (NB5 + NW))

                def split_tokens(k):
                    slot, _, width = blocks[k]
                    dve.wait_ge(h_loaded, quarter * (16 * NB5) + 16 * (k + 1))
                    dve.wait_ge(f_mm, quarter * (NB5 * NF) + NF * (k + 1))
                    split(v, step, h_raw[:, :, 0:width], *parts(slot))
                    dve.sem_inc(h_split, 1)

                def split_weight(g):
                    dve.wait_ge(w_loaded[g], 16 * (quarter + 1))
                    dve.wait_ge(f_mm, quarter * (NB5 * NF) + NF + WGRP * (g + 1))
                    cols = slice(g * WGRP * P, (g + 1) * WGRP * P)
                    split(v, step, w_raw[:, g], w[:, :, cols], wl[:, :, cols])
                    dve.sem_inc(w_split, 1)

                split_tokens(0)
                split_weight(0)
                for k, (_, _, width) in enumerate(blocks):
                    for n in range(NF):
                        at = NF * k + n
                        if k == 0 and n % WGRP == 0 and n // WGRP + 1 < NW:
                            split_weight(n // WGRP + 1)
                        if n == 5 and k + 1 < NB5:
                            split_tokens(k + 1)
                        dve.wait_ge(f_mm, quarter * (NB5 * NF) + 2 * NF + at + 1)
                        g = n // GRP
                        if n % GRP == 0:
                            dve.wait_ge(f_stored[g % 2], quarter * (16 * (NG // 2) * NB5) + 16 * ((NG // 2) * k + g // 2 + 1))
                        p, out = p_f[:, n % 4, 0:width], f[:, g % 2, n % GRP, 0:width]
                        v.tensor_single_scalar(out, p, 0.0, ALU.max).then_inc(rectified, 1)
                        dve.wait_ge(rectified, quarter * (NB5 * NF) + at + 1)
                        v.tensor_tensor(out, out, p, ALU.mult).then_inc(f_out, 1)
                step.end()


def stage_ff2(nc, I, O, S, K):
    NK = FF // P // 2
    NTILE = L // P
    ALL = NTILE + 1
    PAIRS = NTILE // 2
    stores = (PAIRS + 1, PAIRS)
    with Room(nc, "ff2") as r:
        w_raw = r.sb("w_raw", [P, 2, D])
        w = r.sb("w", [P, NK, D], F32R)
        wl = r.sb("wl", [P, NK, D], F32R)
        y_raw = r.sb("y_raw", [P, NK, P])
        y = r.sb("y", [P, 2, NK, P], F32R)
        yl = r.sb("yl", [P, 2, NK, P], F32R)
        x = r.sb("x", [P, 2, D])
        part = r.sb("part", [P, D])
        total = r.sb("total", [P, D])
        squares = r.sb("squares", [P, D])
        gpost = r.sb("gpost", [P, D])
        ss = r.sb("ss", [P, 2])
        p_y = r.ps("p_y", [P, 2, D])
        w_loaded, gain_loaded = r.sems("w_loaded", 2), r.sem("gain_loaded")
        y_loaded, x_loaded = r.pool_sem("y_loaded"), r.pool_sems("x_loaded", 2)
        w_split, y_split, w_used, y_mm, p_free = (r.sem(n) for n in ("w_split", "y_split", "w_used", "y_mm", "p_free"))
        summed, rstd, x_done, s_act = r.sem("summed"), r.sem("rstd"), r.sem("x_done"), r.sem("steps_act")
        stored = r.sems("stored", 2)
        passed, passed_pool, passed_pe = r.sem("passed"), r.sem("passed_pool"), r.sem("passed_pe")
        steps = r.sems("steps", 5)
        block = r.block()

        def tokens(q, rows):
            return slice(L, T) if rows == TS else bass.ds(q * P, P)

        def tiles(engine, body):
            with engine.Fori(0, PAIRS) as i:
                for u in range(2):
                    body(2 * i + u, u, i, P)
            body(NTILE, 0, PAIRS, TS)

        @block.gpsimd
        def _(pool):
            def load_y(half, q, u, rows):
                hold(pool, passed_pool, y_split, q + (half * ALL + 1))
                pool.dma_start(y_raw[:, :, 0:rows], S["ff"][half * NK * P:(half + 1) * NK * P, tokens(q, rows)].rearrange(
                    "(c p) t -> p c t", p=P)).then_inc(y_loaded, 16)

            tiles(pool, lambda q, u, i, rows: load_y(0, q, u, rows))
            for u in range(2):
                pool.wait_ge(stored[u], 16 + 16 * stores[u])

            def second(q, u, i, rows):
                load_y(1, q, u, rows)
                hold(pool, passed_pool, summed, q + 1)
                pool.dma_start(part[0:rows, :], S["ff_part"][tokens(q, rows), :]).then_inc(x_loaded[u], 16)
                hold(pool, passed_pool, stored[u], i * 16 + 16 * (stores[u] + 1))
                pool.dma_start(x[0:rows, u, :], S["x2"][tokens(q, rows), :]).then_inc(x_loaded[u], 16)
            tiles(pool, second)

        @block.sync
        def _(sp):
            for u in range(2):
                sp.sem_inc(stored[u], 16)
            sp.dma_start(gpost[:], I["norms"][5].partition_broadcast(P)).then_inc(gain_loaded, 16)
            sp.wait_ge(y_loaded, 16)

            def load_w(half, c):
                n = half * NK + c
                if n >= 2:
                    sp.wait_ge(w_split, n - 1)
                sp.dma_start(w_raw[:, c % 2, :], I["w_ff2"][n * P:(n + 1) * P, :]).then_inc(w_loaded[c % 2], 16)

            for c in range(NK):
                load_w(0, c)

            def store_sums(q, u, i, rows):
                hold(sp, passed, p_free, q + 3)
                sp.dma_start(S["ff_part"][tokens(q, rows), :], x[0:rows, u, :]).then_inc(stored[u], 16)

            with sp.Fori(0, PAIRS) as i:
                for u in range(2):
                    store_sums(2 * i + u, u, i, P)
            for c in range(NK):
                load_w(1, c)
            store_sums(NTILE, 0, PAIRS, TS)

            def store(q, u, i, rows):
                hold(sp, passed, x_done, q + 1)
                to = O["y_prompt"][tokens(q, rows), :] if rows == P else O["y_sample"]
                sp.dma_start(to, x[0:rows, u, :]).then_inc(stored[u], 16)
            tiles(sp, store)
            for u in range(2):
                sp.wait_ge(stored[u], 16 + 32 * stores[u])

        @block.tensor
        def _(pe):
            pe.sem_inc(y_mm, 2)

            def product(half, q, u, i, rows):
                hold(pe, passed_pe, y_split, q + (half * ALL + 2))
                hold(pe, passed_pe, p_free, q + (half * ALL + 1))
                hy, ly = y[:, u, :, 0:rows], yl[:, u, :, 0:rows]
                for c in range(NK):
                    if u == 0 and rows == P:
                        pe.wait_ge(w_split, half * NK + c + 1)
                    for n in range(2):
                        cols = slice(n * 512, (n + 1) * 512)
                        for yp, wp in ((ly, w), (hy, wl), (hy, w)):
                            last = nc.tensor.matmul(p_y[0:rows, u, cols], yp[:, c, :],
                                                    wp[:, c, cols], start=(c == 0 and yp is ly),
                                                    stop=(c == NK - 1 and yp is hy and wp is w))
                    if rows == TS and half == 0 and c < NK - 1:
                        last.then_inc(w_used, 1)
                last.then_inc(y_mm, 1)

            tiles(pe, lambda *a: product(0, *a))
            pe.wait_ge(p_free, 2 + ALL)
            tiles(pe, lambda *a: product(1, *a))

        @block.scalar
        def _(act):
            nc.scalar.preload_act_table_set(LN_EXP)

            def copy_out(q, u, i, rows):
                act.wait_ge(y_mm, q + 3)
                act.wait_ge(stored[u], i * 16 + 16)
                nc.scalar.activation(x[0:rows, u, :], p_y[0:rows, u, :], ACT.Copy).then_inc(p_free, 1)
            tiles(act, copy_out)

            def scale(q, u, i, rows):
                act.wait_ge(summed, q + 2)
                step = Steps(act, s_act)
                step.start = 3 * q
                step(nc.scalar.activation(squares[0:rows, :], total[0:rows, :], ACT.Square, accum_out=ss[0:rows, 0:1]))
                step(nc.scalar.activation(ss[0:rows, 1:2], ss[0:rows, 0:1], ACT.Ln, scale=1.0 / D, bias=K["eps"][0:rows, :]))
                step(nc.scalar.activation(ss[0:rows, 1:2], ss[0:rows, 1:2], ACT.Exp, scale=-0.5))
                act.sem_inc(rstd, 1)
            tiles(act, scale)

        @block.vector
        def _(dve):
            v = nc.vector
            dve.sem_inc(p_free, 2)
            dve.sem_inc(summed, 1)
            dve.sem_inc(y_split, 1)

            def split_y(step, half, q, u, rows):
                dve.wait_ge(y_loaded, q * 16 + 16 * (half * ALL + 1))
                dve.wait_ge(y_mm, q + (half * ALL + 1))
                split(v, step, y_raw[:, :, 0:rows], y[:, u, :, 0:rows], yl[:, u, :, 0:rows])
                dve.sem_inc(y_split, 1)

            def split_w(step, half):
                for c in range(NK):
                    dve.wait_ge(w_loaded[c % 2], 16 * ((half * NK + c) // 2 + 1))
                    if half:
                        if c < NK - 1:
                            dve.wait_ge(w_used, c + 1)
                        else:
                            dve.wait_ge(y_mm, 2 + ALL)
                    split(v, step, w_raw[:, c % 2, :], w[:, c, :], wl[:, c, :])
                    dve.sem_inc(w_split, 1)

            def finish(step, q, u, i, rows):
                dve.wait_ge(y_mm, q + (2 + ALL + 1))
                dve.wait_ge(x_loaded[u], i * 32 + 32)
                step(v.tensor_tensor(total[0:rows, :], p_y[0:rows, u, :], part[0:rows, :], ALU.add))
                dve.sem_inc(summed, 1)
                dve.sem_inc(p_free, 1)
                dve.wait_ge(rstd, q + 1)
                step(v.scalar_tensor_tensor(out=total[0:rows, :], in0=total[0:rows, :], scalar=ss[0:rows, 1:2],
                                            in1=gpost[0:rows, :], op0=ALU.mult, op1=ALU.mult))
                step(v.tensor_tensor(x[0:rows, u, :], x[0:rows, u, :], total[0:rows, :], ALU.add))
                dve.sem_inc(x_done, 1)

            def pass_by(half, step0, in_loop, after):
                if half:
                    split_w(step0, half)
                    split_y(step0, half, 0, 0, P)
                else:
                    split_y(step0, half, 0, 0, P)
                    split_w(step0, half)
                per = 4 + (6 if half else 0)
                with dve.Fori(0, PAIRS - 1) as i:
                    step = Steps(dve, in_loop, i, per)
                    for u in range(2):
                        split_y(step, half, 2 * i + (u + 1), 1 - u, P)
                        if half:
                            finish(step, 2 * i + u, u, i, P)
                    step.end()
                for u in range(2):
                    split_y(after, half, NTILE - 1 + u, 1 - u, P if u == 0 else TS)
                    if half:
                        finish(after, NTILE - 2 + u, u, PAIRS - 1, P)
                if half:
                    finish(after, NTILE, 0, PAIRS, TS)

            pass_by(0, Steps(dve, steps[0]), steps[1], Steps(dve, steps[2]))
            dve.wait_ge(gain_loaded, 16)
            pass_by(1, Steps(dve, steps[3]), steps[4], Steps(dve, steps[2], 1, 4))


class Cache:

    def __init__(self, tiles, k_load, k_cols, v_load, halves, paged, new):
        self.tiles, self.k_load, self.k_cols, self.v_load = tiles, k_load, k_cols, v_load
        self.halves, self.paged, self.new = halves, paged, new
        self.group = min(4, tiles)
        self.groups = tiles // self.group
        self.rows = P if halves == 2 else HD


CACHES = {
    "fox": Cache(NPAGE, (0, 256), (0, 256), (256, 512), 2, True, True),
    "sel": Cache(NPAGE, (0, 256), (128, 192), (192, 256), 1, True, True),
    "win": Cache(WIN // P, (0, 64), (0, 64), (64, 128), 1, False, True),
    "xa": Cache(MEM // P, (0, 256), (0, 256), (256, 512), 2, False, False),
}


def stage_sample(nc, I, O, S, K, kind):
    C = CACHES[kind]
    G, NG, NP_, H2, R = C.group, C.groups, C.tiles, C.halves, C.rows
    W = H2 * P
    KEYS = NP_ * P
    NEWK = TS if C.new else 0
    KC0, VC = C.k_load[1] - C.k_load[0], C.v_load[1] - C.v_load[0]
    SLOT = min(2, NG)
    paged, fox, sel = C.paged, kind == "fox", kind == "sel"
    src = {"fox": I["cache_fox_kv"], "sel": I["cache_nsa_kv"], "win": I["state_nsa_win"], "xa": I["cache_xa_kv"]}[kind]
    with Room(nc, "smp_" + kind) as r:
        pt = r.sb("pt", [1, NB * NPAGE], I32)
        qT = r.sb("qT", [R, H2 if H2 == 2 else NH, TS])
        qp = r.sb("qp", [R, NB * W + 4 * NB + W])
        qall = r.sb("qall", [R, H2, P])
        qb = r.sb("qb", [R, W])
        kb = r.sb("kb", [P, NP_, KC0])
        kT = r.sb("kT", [R, SLOT, H2, G * P])
        s = r.sb("s", [P, KEYS + NEWK])
        m = r.sb("m", [P, 4])
        pT = r.sb("pT", [P, NP_ + 1, P])
        NVB = NB // 2
        vb = r.sb("vb", [P, NVB, NP_, VC])
        oT = r.sb("oT", [R, H2 if H2 == 2 else NH, TS])
        p_s = r.ps("p_s", [P, 4, 512])
        p_x = [r.ps(f"p_x{k}", [P, 512]) for k in range(4)]
        if C.new:
            knT = r.sb("knT", [R, H2, TS])
            vn = r.sb("vn", [P, VC])
            one32 = r.sb("one32", [TS, TS])
            mnew = r.sb("mnew", [P, TS])
        if fox:
            lrow = r.sb("lrow", [NB, NPAGE, PAGE, NH])
            csum = r.sb("csum", [NB, NH, PAST])
            one8 = r.sb("one8", [NB, PAST])
            nc_all = r.sb("nc_all", [P, PAST])
            lnew = r.sb("lnew", [TS, NH])
            lrep = r.sb("lrep", [TS, NH, TS])
            tri = r.sb("tri", [TS, TS])
        if sel:
            wrep = r.sb("wrep", [P, P])
            ind = r.sb("ind", [P, 4])
            prod = r.sb("prod", [P, G, P])
            kvc = r.sb("kvc", [P, NB, HD])
            pc = r.sb("pc", [P, HD])
            pcT = r.sb("pcT", [HD, P])
            gsum = r.sb("gsum", [P, P])
            imp = r.sb("imp", [P, 33])
            best, work, off, sb_ = r.sb("best", [P, 8]), r.sb("work", [P, 33]), r.sb("off", [P, 33]), r.sb("sbias", [P, 33])
            vcb = r.sb("vcb", [HD, NB, P])
            ocT = r.sb("ocT", [HD, P])
        winb = r.sb("winb", [P, 4])
        zero, zero4 = r.sb("zero", [P, P]), r.sb("zero4", [P, 512])
        lf_rows, lf_sums = S["lf_rows"], S["lf_sums"]
        NMASK = 8 if fox else 4 if C.new else 0
        PT0 = 2 if sel else 1
        PE0 = {"fox": 1, "sel": 5, "win": 1, "xa": 0}[kind]
        pt_loaded, consts = r.sem("pt_loaded"), r.sem("consts")
        by_pool = [paged and g % 2 == 1 for g in range(NG)]
        k_loaded = [(r.pool_sem if by_pool[g] else r.sem)(f"k_loaded{g}") for g in range(NG)]
        passed_pool = r.sem("passed_pool")
        v_loaded = r.sems("v_loaded", NVB)
        passed, passed_dve, passed_pe, turned, kT_done, scored, qb_done, zeroed = (r.sem(n) for n in (
            "passed", "passed_dve", "passed_pe", "turned", "kT_done", "scored", "qb_done", "zeroed"))
        prod_done, cmp_mm, cmp_out, steps, masks, setup = (r.sem(n) for n in (
            "prod_done", "cmp_mm", "cmp_out", "steps", "masks", "setup"))
        to_pe, from_pe, to_act, from_act, o_mm, o_out, stored, lf_back = (r.sem(n) for n in (
            "to_pe", "from_pe", "to_act", "from_act", "o_mm", "o_out", "stored", "lf_back"))
        lf_loaded = r.pool_sem("lf_loaded") if fox else None
        lf_loaded_act = r.sem("lf_loaded_act")
        block = r.block()

        def tile_rows(eng, b, p):
            if paged:
                page = eng.value_load(pt[0:1, bass.ds(b * NPAGE + p, 1)], min_val=0, max_val=159)
                return src[bass.ds(page, 1), :, :].rearrange("o p n -> (o p) n")
            return src[bass.ds(b, 1), p * P:(p + 1) * P, :].rearrange("o p n -> (o p) n")

        def load_tiles(eng, dst, b, p0, p1, columns, sem):
            if paged:
                for p in range(p0, p1):
                    eng.dma_start(dst[:, p, :], tile_rows(eng, b, p)[:, columns[0]:columns[1]]).then_inc(sem, 16)
            else:
                rows = src[bass.ds(b, 1), p0 * P:p1 * P, columns[0]:columns[1]]
                eng.dma_start(dst[:, p0:p1, :], rows.rearrange("o (t p) n -> p (o t) n", p=P)).then_inc(sem, 16)

        def load_forget(eng, b, p0, p1, sem):
            for p in range(p0, p1):
                page = eng.value_load(pt[0:1, bass.ds(b * NPAGE + p, 1)], min_val=0, max_val=159)
                eng.dma_start(lf_rows[bass.ds(b, 1), p * PAGE * NH:(p + 1) * PAGE * NH],
                              I["cache_fox_logf"][bass.ds(page, 1), :, :].rearrange("o p h -> o (p h)")
                              ).then_inc(sem, 16)

        def load_keys(eng, b, g, pass_sem):
            hold(eng, pass_sem, turned, NG * b + g + 1)
            if sel:
                hold(eng, pass_sem, prod_done, NG * b + g + 1)
            load_tiles(eng, kb, b, g * G, (g + 1) * G, C.k_load, k_loaded[g])

        def load_late_values(eng, ks):
            for k in ks:
                eng.wait_ge(o_mm, k + 1)
                load_tiles(eng, vb[:, k], NVB + k, 0, NP_, C.v_load, v_loaded[k])

        KLOADS = G if paged else 1
        VLOADS = NP_ if paged else 1

        NCONST = 1 + (2 if C.new else 0) + (1 if fox else 0) + (8 if sel else 0)
        q_src = {"fox": S["feat"][R_FQ:R_FQ + GW, L:T], "xa": S["xa_q"][:, L:T]}.get(kind, S["feat"][R_NQ:R_NQ + GW, L:T])
        g_out = {"fox": S["group"][G_FOX:G_FOX + GW, L:T], "sel": S["group"][G_SEL:G_SEL + GW, L:T],
                 "win": S["group"][G_WIN:G_WIN + GW, L:T], "xa": S["xa_o"][:, L:T]}[kind]
        fold = "(c p) t -> p c t"

        @block.sync
        def _(sp):
            sp.dma_start(pt[:], I["page_table"]).then_inc(pt_loaded, 16)
            sp.dma_start(qT[:], q_src.rearrange(fold, p=R)).then_inc(consts, 16)
            if C.new:
                kr = {"fox": R_FK, "sel": R_KS, "win": R_KW}[kind]
                sp.dma_start(knT[:], S["feat"][kr:kr + H2 * R, L:T].rearrange(fold, p=R)).then_inc(consts, 16)
                vnew = {"fox": O["fox_kv_s"][:, 256:512], "sel": O["nsa_kv_s"][:, 192:256],
                        "win": S["win_kv"][L:T, 64:128]}[kind]
                sp.dma_start(vn[0:TS, :], vnew).then_inc(consts, 16)
            if fox:
                sp.dma_start(lnew[:], O["fox_logf_s"]).then_inc(consts, 16)
            if sel:
                for n in range(4):
                    for kv in range(2):
                        sp.dma_start(wrep[32 * n:32 * n + 32, kv * HD:(kv + 1) * HD], I["nsa_cmp_w"][kv]).then_inc(consts, 16)
            sp.wait_ge(pt_loaded, 16)
            with sp.Fori(0, NB) as b:
                for g in range(NG):
                    if not by_pool[g]:
                        load_keys(sp, b, g, passed)
            load_late_values(sp, (1, 3))
            sp.wait_ge(o_out, NB + 1)
            sp.dma_start(g_out.rearrange(fold, p=R), oT[:]).then_inc(stored, 16)
            n = 1
            if sel:
                sp.dma_start(S["group"][G_CMP:G_CMP + GW, L:T].rearrange("(h d) t -> d h t", h=NH),
                             ocT[:].rearrange("d (h t) -> d h t", h=NH)).then_inc(stored, 16)
                n += 1
            if kind == "win":
                for b in range(NB):
                    sp.dma_start(O["nsa_win_s"][b, 0:WIN - NT, :], I["state_nsa_win"][b, NT:WIN, :]).then_inc(stored, 16)
                    sp.dma_start(O["nsa_win_s"][b, WIN - NT:WIN, :],
                                 S["win_kv"][L + NT * b:L + NT * (b + 1), :]).then_inc(stored, 16)
                    n += 2
            sp.wait_ge(stored, 16 * n)

        @block.gpsimd
        def _(pool):
            st = Steps(pool, masks)
            if C.new:
                st(nc.gpsimd.memset(one32[:], 1.0))
                v3 = one32[:].rearrange("p (b j) -> p b j", j=NT)
                for pat, base, mult in (([[-NT, NB], [0, NT]], 0, 1), ([[NT, NB], [0, NT]], NT - 1, -1),
                                        ([[-NT, NB], [-1, NT]], 0, 1)):
                    st(nc.gpsimd.affine_select(out=v3, in_=v3, pattern=pat, base=base, channel_multiplier=mult,
                                               compare_op=ALU.is_ge, fill=0.0))
            if fox:
                st(nc.gpsimd.memset(tri[:], -1.0))
                v3 = tri[:].rearrange("p (b j) -> p b j", j=NT)
                for pat, base, mult in (([[-NT, NB], [0, NT]], 0, 1), ([[NT, NB], [0, NT]], NT - 1, -1),
                                        ([[NT, NB], [1, NT]], 0, -1)):
                    st(nc.gpsimd.affine_select(out=v3, in_=v3, pattern=pat, base=base, channel_multiplier=mult,
                                               compare_op=ALU.is_ge, fill=0.0))
            if paged:
                pool.wait_ge(pt_loaded, 16)
                with pool.Fori(0, NB) as b:
                    for g in range(NG):
                        if by_pool[g]:
                            load_keys(pool, b, g, passed_pool)
                    if fox:
                        load_forget(pool, b, 0, NPAGE // 2, lf_loaded)
            if fox:
                pool.wait_ge(lf_loaded, 16 * (NB // 2) * NPAGE)
                pool.wait_ge(lf_loaded_act, 16 * (NB // 2) * NPAGE)
                pool.dma_start(lrow[:].rearrange("b p k h -> b (p k h)"), lf_rows).then_inc(lf_loaded, 16)
                pool.wait_ge(lf_back, 1)
                pool.dma_start(lf_sums, csum[:]).then_inc(lf_loaded, 16)
                pool.wait_ge(lf_loaded, 16 * (NB // 2 * NPAGE + 2))
                for h in range(NH):
                    pool.dma_start(nc_all[h * TS:(h + 1) * TS, :], bc(lf_sums[:, h, :], 1, NT)).then_inc(lf_loaded, 16)
            nmasks = st.n
            assert nmasks == NMASK

        @block.tensor
        def _(pe):
            mm = nc.tensor.matmul
            pe.sem_inc(turned, NG)
            pe.sem_inc(scored, SLOT)
            if sel:
                pe.sem_inc(cmp_mm, 1)
            NK = (KEYS + 511) // 512
            width = min(512, KEYS)
            pe.wait_ge(setup, 1)
            for n in range(NK):
                mm(p_s[:, n, 0:width], zero[:], zero4[:, 0:width],
                   start=True, stop=False, skip_group_check=True).then_inc(zeroed, 1)
            with pe.Fori(0, NB) as b:
                def turn(g):
                    hold(pe, passed_pe, k_loaded[g], 16 * KLOADS * (b + 1))
                    hold(pe, passed_pe, kT_done, NG * b + g + 1)
                    for p in range(G):
                        for c in range(H2):
                            k0 = C.k_cols[0] + c * P
                            last = nc.tensor.transpose(p_x[2 * (g % 2) + c][0:R, p * P:(p + 1) * P],
                                                       kb[:, g * G + p, k0:k0 + R], K["ident"][:])
                    last.then_inc(turned, 1)

                def compress(g):
                    pe.wait_ge(prod_done, NG + NG * b + g + 1)
                    if g == 0:
                        pe.wait_ge(cmp_out, b + 1)
                    for p in range(G):
                        last = mm(p_x[1][:, (g * G + p) * 4:(g * G + p + 1) * 4], prod[:, p, :], ind[:], start=True,
                                  stop=True)
                    last.then_inc(cmp_mm, 1)

                def score(g):
                    pe.wait_ge(kT_done, SLOT + NG * b + g + 1)
                    pe.wait_ge(qb_done, b + 1)
                    for c in range(H2):
                        last = mm(p_s[:, g, 0:width], qb[:, c * P:(c + 1) * P], kT[:, g % 2, c, :], start=False,
                                  stop=False, skip_group_check=True)
                    last.then_inc(scored, 1)

                turn(0)
                for g in range(NG):
                    if g + 1 < NG:
                        turn(g + 1)
                    if sel:
                        compress(g)
                    score(g)
            todo = [0]

            def asked():
                todo[0] += 1
                pe.wait_ge(to_pe, todo[0])

            if C.new:
                asked()
                for c in range(H2):
                    lhs = qall[:, c, :]
                    last = mm(p_x[0][:, 0:TS], lhs, knT[:, c, :], start=(c == 0), stop=(c == H2 - 1 and not fox))
                if fox:
                    last = mm(p_x[0][:, 0:TS], lrep[:].rearrange("p h q -> p (h q)"), tri[:], start=False, stop=True)
                last.then_inc(from_pe, 1)
            if sel:
                asked()
                for b in range(NB):
                    last = mm(p_x[1][:, 0:HD], qp[:, b * W:b * W + P], kvc[0:HD, b, :], start=(b == 0), stop=(b == NB - 1))
                last.then_inc(from_pe, 1)
                asked()
                mm(p_x[2][:, 0:HD], gsum[:], pc[:], start=True, stop=True)
                nc.tensor.transpose(p_x[3][0:HD, 0:P], pc[:], K["ident"][:]).then_inc(from_pe, 1)
                asked()
                for b in range(NB):
                    last = nc.tensor.transpose(p_x[1 + b // 4][0:HD, (b % 4) * P:(b % 4 + 1) * P], kvc[:, b, :],
                                               K["ident"][:])
                last.then_inc(from_pe, 1)
                asked()
                for b in range(NB):
                    last = mm(p_x[3][0:HD, 0:P].rearrange("d (h b t) -> d h b t", h=NH, b=NB)[:, :, b, :],
                              vcb[:, b, HD:P], pcT[:].rearrange("n (h b t) -> n h b t", h=NH, b=NB)[:, :, b, :],
                              start=True, stop=True)
                last.then_inc(from_pe, 1)
            asked()
            NT_ = NP_ + (1 if C.new else 0)
            for p in range(NT_):
                w = P if p < NP_ else TS
                if p % 4 == 0 and p >= 8:
                    pe.wait_ge(from_act, PT0 + p // 4 - 1)
                last = nc.tensor.transpose(p_x[(p // 4) % 2][0:w, (p % 4) * P:(p % 4 + 1) * P],
                                           s[:, p * P:p * P + w], K["ident"][:])
                if p % 4 == 3 or p == NT_ - 1:
                    last.then_inc(from_pe, 1)
            pe.wait_ge(from_act, PT0 + (NT_ + 3) // 4)

            def cols(b, p, c):
                t = pT[:, p, :].rearrange("k (h q) -> k h q", h=NH)
                return (t[:, 2 * c:2 * c + 2, bass.ds(b * NT, NT)] if H2 == 2 else t[:, :, bass.ds(b * NT, NT)])

            ncol = 2 * NT if H2 == 2 else NH * NT
            with pe.Fori(0, NB // NVB) as i:
                for k in range(NVB):
                    b = i * NVB + k
                    hold(pe, passed_pe, o_out, b + 1)
                    hold(pe, passed_pe, v_loaded[k], 16 * VLOADS * (i + 1))
                    for p in range(NP_):
                        for c in range(H2):
                            last = mm(p_x[2 + c][0:R, 0:ncol], vb[:, k, p, c * P:c * P + R], cols(b, p, c), start=(p == 0),
                                      stop=(p == NP_ - 1 and not C.new))
                    if C.new:
                        for c in range(H2):
                            last = mm(p_x[2 + c][0:R, 0:ncol], vn[:, c * P:c * P + R], cols(b, NP_, c), start=False, stop=True)
                    last.then_inc(o_mm, 1)

        @block.scalar
        def _(act):
            nc.scalar.preload_act_table_set(LN_EXP)
            a = nc.scalar
            act.wait_ge(pt_loaded, 16)
            if fox:
                with act.Fori(0, NB) as b:
                    load_forget(act, b, NPAGE // 2, NPAGE, lf_loaded_act)

            for k in range(NVB):
                load_tiles(act, vb[:, k], k, 0, NP_, C.v_load, v_loaded[k])
            n = 0
            if sel:
                act.wait_ge(to_act, 1)
                a.activation(pc[:], pc[:], ACT.Exp, bias=m[:, 0:1], accum_out=m[:, 1:2]).then_inc(from_act, 1)
                n = 1
            act.wait_ge(to_act, n + 1)
            a.activation(s[:], s[:], ACT.Exp, bias=m[:, 0:1], accum_out=m[:, 1:2]).then_inc(from_act, 1)
            NT_ = NP_ + (1 if C.new else 0)
            for k in range((NT_ + 3) // 4):
                cnt = min(4, NT_ - 4 * k)
                act.wait_ge(from_pe, PE0 + k + 1)
                if C.new and k == (NT_ - 1) // 4:
                    if cnt > 1:
                        a.activation(pT[:, 4 * k:4 * k + cnt - 1, :],
                                     p_x[k % 2][:, 0:(cnt - 1) * P].rearrange("p (n q) -> p n q", q=P), ACT.Copy)
                    a.activation(pT[0:TS, NP_, :], p_x[k % 2][0:TS, (cnt - 1) * P:cnt * P], ACT.Copy).then_inc(from_act, 1)
                else:
                    a.activation(pT[:, 4 * k:4 * k + cnt, :], p_x[k % 2][:, 0:cnt * P].rearrange("p (n q) -> p n q", q=P),
                                 ACT.Copy).then_inc(from_act, 1)
            load_late_values(act, (0, 2))

        @block.vector
        def _(dve):
            v = nc.vector
            step = Steps(dve, steps)
            dve.sem_inc(kT_done, SLOT)
            dve.sem_inc(o_out, 1)
            v.memset(zero[:], 0.0)
            if C.new:
                for rows in (slice(TS, 2 * TS), slice(2 * TS, P)):
                    v.memset(vn[rows, :], 0.0)
                    v.memset(pT[rows, NP_, :], 0.0)
            v.memset(zero4[:], 0.0).then_inc(setup, 1)
            step(v.memset(qp[:], 0.0))
            step(v.memset(qall[:], 0.0))
            dve.wait_ge(consts, 16 * NCONST)
            for h in range(NH):
                if H2 == 2:
                    c, half = h // 2, HD * (h % 2)
                    rows, srcq = slice(half, half + HD), qT[half:half + HD, c, :]
                    o0 = c * P + h * TS
                    v.tensor_copy(qall[rows, c, h * TS:(h + 1) * TS], srcq)
                else:
                    rows, srcq, o0 = slice(0, HD), qT[:, h, :], h * TS
                    v.tensor_copy(qall[rows, 0, h * TS:(h + 1) * TS], srcq)
                dst = qp[rows, o0:o0 + NB * (W + NT)].rearrange("p (b w) -> p b w", w=W + NT)[:, :, 0:NT]
                last = v.tensor_copy(dst, srcq.rearrange("p (b t) -> p b t", t=NT))
            step(last)
            if C.new:
                dve.wait_ge(masks, NMASK)
                for h in range(NH):
                    last = v.tensor_scalar(mnew[h * TS:(h + 1) * TS, :], one32[:], -NEG, NEG, ALU.mult, ALU.add)
                if kind == "win":
                    for h in range(NH):
                        last = v.tensor_reduce(winb[h * TS:(h + 1) * TS, :], one32[:].rearrange("p (b j) -> p j b", j=NT),
                                               AX.X, ALU.add)
                step(last)
                if kind == "win":
                    step(v.tensor_single_scalar(winb[:], winb[:], NEG, ALU.mult))
            if fox:
                step(v.tensor_copy(lrep[:], bc(lnew[:], 2, TS)))
                v.memset(one8[:], 1.0)
            if sel:
                step(v.memset(ind[:], 0.0))
                for n in range(4):
                    last = v.memset(ind[32 * n:32 * n + 32, n:n + 1], 1.0)
                for n in range(4):
                    last = v.tensor_copy(gsum[32 * n:32 * n + 32, :].rearrange("p (h q) -> p h q", h=NH),
                                         bc(K["ident"][0:32, 0:32], 1, NH))
                step(last)
                dve.sem_inc(prod_done, NG)
                dve.sem_inc(cmp_out, 1)
            with dve.Fori(0, NB) as b:
                dve.wait_ge(scored, SLOT + NG * b)
                v.tensor_copy(qb[:], qp[:, bass.ds(b * W, W)]).then_inc(qb_done, 1)
                for g in range(NG):
                    if sel:
                        dve.wait_ge(k_loaded[g], 16 * KLOADS * (b + 1))
                        dve.wait_ge(cmp_mm, 1 + NG * b + g)
                        v.tensor_tensor(prod[:], kb[:, g * G:(g + 1) * G, 0:P], bc(wrep[:], 1, G),
                                        ALU.mult).then_inc(prod_done, 1)
                    dve.wait_ge(turned, NG + NG * b + g + 1)
                    dve.wait_ge(scored, NG * b + g + 1)
                    for c in range(H2):
                        last = v.tensor_copy(kT[:, g % 2, c, :], p_x[2 * (g % 2) + c][0:R, 0:G * P])
                    last.then_inc(kT_done, 1)
                if sel:
                    dve.wait_ge(cmp_mm, 1 + NG * b + NG)
                    v.tensor_copy(kvc[:, bass.ds(b, 1), :], bc(p_x[1][:, 0:HD], 1, 1)).then_inc(cmp_out, 1)

            pe_n, act_n = [0], [0]

            def ask_pe():
                pe_n[0] += 1
                dve.sem_inc(to_pe, 1)
                return pe_n[0]

            if fox:
                dve.wait_ge(lf_loaded, 16 * (NB // 2 * NPAGE + 1))
                for h in range(NH):
                    last = v.tensor_tensor_scan(csum[:, h, :], one8[:], lrow[:].rearrange("b p k h -> b (p k) h")[:, :, h],
                                                0.0, ALU.mult, ALU.subtract)
                step(last)
                dve.sem_inc(lf_back, 1)
            dve.wait_ge(scored, SLOT + NG * NB)
            dve.wait_ge(kT_done, SLOT + NG * NB)
            past = s[:, 0:KEYS]
            if C.new:
                ask_pe()
            if sel:
                dve.wait_ge(cmp_out, 1 + NB)
                ask_pe()
                dve.wait_ge(from_pe, 2)
                step(v.tensor_copy(pc[:], p_x[1][:, 0:HD]))
                step(v.tensor_reduce(m[:, 2:3], pc[:], AX.X, ALU.max))
                step(v.tensor_single_scalar(m[:, 0:1], m[:, 2:3], -1.0, ALU.mult))
                dve.sem_inc(to_act, 1)
                dve.wait_ge(from_act, 1)
                step(v.reciprocal(m[:, 3:4], m[:, 1:2]))
                step(v.tensor_scalar(pc[:], pc[:], m[:, 3:4], None, ALU.mult))
                ask_pe()
                dve.wait_ge(from_pe, 3)
                v.tensor_reduce(imp[:, 0:32], p_x[2][:, 0:HD].rearrange("p (b r) -> p b r", r=2), AX.X, ALU.add)
                step(v.tensor_copy(pcT[:], p_x[3][0:HD, 0:P]))
                ask_pe()
                v.memset(imp[:, 0:1], 1e9)
                step(v.memset(imp[:, 32:33], 1e9))
                top16(v, step, passed_dve, imp[:], best[:], work[:], off[:], sb_[:])
                dve.wait_ge(from_pe, 4)
                for n in range(2):
                    last = v.tensor_copy(vcb[:, 4 * n:4 * n + 4, :], p_x[1 + n][0:HD, :].rearrange("p (b q) -> p b q", q=P))
                step(last)
                ask_pe()
                dve.wait_ge(from_pe, 5)
                step(v.tensor_copy(ocT[:], p_x[3][0:HD, 0:P]))
                v.tensor_tensor(past.rearrange("p (b j) -> p b j", j=64),
                                p_s[:].rearrange("p a (b j) -> p (a b) j", j=64), bc(sb_[:, 0:32], 2, 64), ALU.add)
                step(v.scalar_tensor_tensor(out=s[:, KEYS:], in0=p_x[0][:, 0:TS], scalar=sb_[:, 32:33], in1=mnew[:],
                                            op0=ALU.add, op1=ALU.add))
            elif fox:
                dve.wait_ge(from_pe, 1)
                dve.wait_ge(lf_loaded, 16 * (NB // 2 * NPAGE + 2 + NH))
                v.tensor_tensor(past, p_s[:].rearrange("p a b -> p (a b)"), nc_all[:], ALU.add)
                step(v.scalar_tensor_tensor(out=s[:, KEYS:], in0=p_x[0][:, 0:TS], scalar=nc_all[:, PAST - 1:PAST],
                                            in1=mnew[:], op0=ALU.add, op1=ALU.add))
            elif kind == "win":
                dve.wait_ge(from_pe, 1)
                v.tensor_copy(past, p_s[:, 0, :])
                step(v.tensor_tensor(s[:, KEYS:], p_x[0][:, 0:TS], mnew[:], ALU.add))
                step(v.tensor_tensor(s[:, 0:NT], s[:, 0:NT], winb[:], ALU.add))
            else:
                step(v.tensor_copy(past, p_s[:, 0, 0:KEYS]))
            step(v.tensor_reduce(m[:, 2:3], s[:], AX.X, ALU.max))
            step(v.tensor_single_scalar(m[:, 0:1], m[:, 2:3], -1.0, ALU.mult))
            dve.sem_inc(to_act, 1)
            dve.wait_ge(from_act, PT0)
            step(v.reciprocal(m[:, 3:4], m[:, 1:2]))
            step(v.tensor_scalar(s[:], s[:], m[:, 3:4], None, ALU.mult))
            ask_pe()
            with dve.Fori(0, NB) as b:
                dve.wait_ge(o_mm, b + 1)
                if H2 == 2:
                    for half in range(2):
                        rows = slice(half * HD, (half + 1) * HD)
                        for c in range(2):
                            last = v.tensor_copy(oT[rows, c, bass.ds(b * NT, NT)],
                                                 p_x[2 + c][rows, half * NT:(half + 1) * NT])
                else:
                    last = v.tensor_copy(oT[:, :, bass.ds(b * NT, NT)],
                                         p_x[2][0:HD, 0:NH * NT].rearrange("d (h t) -> d h t", h=NH))
                last.then_inc(o_out, 1)


def stage_sample_fox(nc, I, O, S, K):
    stage_sample(nc, I, O, S, K, "fox")


def stage_sample_sel(nc, I, O, S, K):
    stage_sample(nc, I, O, S, K, "sel")


def stage_sample_win(nc, I, O, S, K):
    stage_sample(nc, I, O, S, K, "win")


def stage_sample_xa(nc, I, O, S, K):
    stage_sample(nc, I, O, S, K, "xa")


def stage_sample_hgrn(nc, I, O, S, K):
    levels = (2, 1)
    NL = len(levels)
    with Room(nc, "smp_hgrn") as r:
        z = r.sb("z", [P, 3, 2, TS])
        a = r.sb("a", [P, 3, 2, TS])
        b = r.sb("b", [P, 2, TS])
        tmp = r.sb("tmp", [P, 2, TS])
        eb = r.sb("eb", [P, 2, TS])
        ex = r.sb("ex", [P, NL + 1, 2, TS])
        qe = r.sb("qe", [P, NL + 1, 2, TS])
        ke = r.sb("ke", [P, NL + 1, 2, TS])
        qb = r.sb("qb", [P, 2, TS])
        once = r.sb("once", [P, TS])
        mask = r.sb("mask", [TS, NL + 1, TS])
        am = r.sb("am", [TS, NH, NL + 1, TS])
        v = r.sb("v", [TS, GW])
        vm = r.sb("vm", [TS, NB, GW])
        own = r.sb("own", [TS, NB])
        kdT = r.sb("kdT", [TS, 2 * P])
        st = r.sb("st", [P, 2, NB, HD])
        std = r.sb("std", [P, 2, NB, HD])
        o = r.sb("o", [P, 2, TS])
        oi = r.sb("oi", [P, 2, TS])
        sq = r.sb("sq", [P, 2, TS])
        p_a = [r.ps(f"p_a{n}", [P, 512]) for n in range(2)]
        p_t = r.ps("p_t", [P, 512])
        p_i = r.ps("p_i", [P, 512])
        p_j = r.ps("p_j", [P, 512])
        p_u = r.ps("p_u", [P, 2, 512])
        p_r = r.ps("p_r", [P, 512])
        loaded, masks, steps, to_act, from_act, to_pe, from_pe, done, stored = (r.sem(n) for n in (
            "loaded", "masks", "steps", "to_act", "from_act", "to_pe", "from_pe", "done", "stored"))
        low, gain, gates_dve, gates_act = hgrn_gates(nc, nc.scalar, nc.vector, r, z, a, b, tmp, (loaded, 16 * 11), TS)
        block = r.block()

        @block.sync
        def _(sp):
            for n, row in enumerate((R_HQ, R_HF, R_HG)):
                for c in range(2):
                    sp.dma_start(z[:, n, c, :], S["feat"][row + c * P:row + (c + 1) * P, L:T]).then_inc(loaded, 16)
            sp.dma_start(low[:], I["hgrn_lower"].rearrange("(c p) -> p c", p=P),
                         allow_slow_non_contiguous=True).then_inc(loaded, 16)
            sp.dma_start(gain[:], I["g_mix"][GW:2 * GW].rearrange("(c p) -> p c", p=P),
                         allow_slow_non_contiguous=True).then_inc(loaded, 16)
            sp.dma_start(v[:], S["hgrn_v"][L:T, :]).then_inc(loaded, 16)
            state = [t.rearrange("b (c h) k v -> c (h k) b v", c=2) for t in (I["state_hgrn"], O["hgrn_s"])]
            for c in range(2):
                sp.dma_start(st[:, c], state[0][c]).then_inc(loaded, 16)
            sp.wait_ge(done, 1)
            for c in range(2):
                sp.dma_start(state[1][c], st[:, c]).then_inc(stored, 16)
            sp.wait_ge(done, 2)
            for c in range(2):
                sp.dma_start(S["group"][G_HGRN + c * P:G_HGRN + (c + 1) * P, L:T], o[:, c, :]).then_inc(stored, 16)
            sp.wait_ge(stored, 64)

        @block.gpsimd
        def _(pool):
            g = nc.gpsimd
            step = Steps(pool, masks)
            step(g.memset(mask[:], 1.0))
            step(g.memset(own[:], 1.0))
            for l, m in enumerate(levels):
                n = TS // (2 * m)
                view = mask[:, l, :].rearrange("p (n w) -> p n w", w=2 * m)
                for pattern, base, mult in (([[0, n], [1, 2 * m]], -m, 0), ([[-2 * m, n], [0, 2 * m]], 0, 1),
                                            ([[2 * m, n], [0, 2 * m]], m - 1, -1)):
                    step(g.affine_select(out=view, in_=view, pattern=pattern, base=base, channel_multiplier=mult,
                                         compare_op=ALU.is_ge, fill=0.0))
            step(g.affine_select(out=mask[:, NL, :], in_=mask[:, NL, :], pattern=[[-1, TS]], base=0,
                                 channel_multiplier=1, compare_op=ALU.is_equal, fill=0.0))
            step(g.affine_select(out=own[:], in_=own[:], pattern=[[-NT, NB]], base=0, channel_multiplier=1,
                                 compare_op=ALU.is_ge, fill=0.0))
            step(g.affine_select(out=own[:], in_=own[:], pattern=[[NT, NB]], base=NT - 1, channel_multiplier=-1,
                                 compare_op=ALU.is_ge, fill=0.0))
            assert step.n == 11

        @block.scalar
        def _(act):
            nc.scalar.preload_act_table_set(LN_EXP)
            s = nc.scalar
            step = gates_act()
            act.wait_ge(to_act, 1)
            step(s.activation(ex[:], ex[:], ACT.Abs))
            s.activation(eb[:], b[:], ACT.Exp)
            step(s.activation(ex[:], ex[:], ACT.Exp, scale=-1.0))
            act.sem_inc(from_act, 1)
            act.wait_ge(from_pe, 3)
            step(s.activation(eb[:], p_r[:, 0:2 * TS].rearrange("p (c t) -> p c t", c=2), ACT.Ln, scale=1.0 / HD,
                              bias=K["eps"][:]))
            step(s.activation(eb[:], eb[:], ACT.Exp, scale=-0.5))
            act.sem_inc(from_act, 1)

        @block.vector
        def _(dve):
            w = nc.vector
            step = gates_dve()
            w.memset(once[:].rearrange("p (n t) -> p n t", t=NT)[:, :, 1:NT], 1.0)
            step(w.memset(once[:].rearrange("p (n t) -> p n t", t=NT)[:, :, 0:1], 0.0))
            for c in range(2):
                step(w.tensor_tensor_scan(b[:, c, :], once[:], b[:, c, :], 0.0, ALU.mult, ALU.add))
            for l, m in enumerate(levels):
                n = TS // (2 * m)
                bv = b[:].rearrange("p c (n w) -> p c n w", w=2 * m)
                w.tensor_tensor(ex[:, l].rearrange("p c (n w) -> p c n w", w=2 * m), bv,
                                bv[:, :, :, m - 1:m].broadcast_to([P, 2, n, 2 * m]), ALU.subtract)
            bv = b[:].rearrange("p c (n w) -> p c n w", w=NT)
            step(w.tensor_tensor(ex[:, NL].rearrange("p c (n w) -> p c n w", w=NT), bv,
                                 bv[:, :, :, NT - 1:NT].broadcast_to([P, 2, NB, NT]), ALU.subtract))
            dve.sem_inc(to_act, 1)
            dve.wait_ge(masks, 11)
            for n in range(NB):
                w.tensor_scalar(vm[:, n, :], v[:], own[:, n:n + 1], None, ALU.mult)
            dve.wait_ge(from_act, 1)
            qj, kj = z[:, 0], z[:, 1]
            w.tensor_tensor(qb[:], qj, eb[:], ALU.mult)
            w.tensor_tensor(qe[:, 0:NL], ex[:, 0:NL], bc(qj, 1, NL), ALU.mult)
            w.tensor_copy(qe[:, NL], qj)
            w.tensor_tensor(ke[:, 0:NL], ex[:, 0:NL], bc(kj, 1, NL), ALU.mult)
            w.tensor_tensor(ex[:, NL], ex[:, NL], kj, ALU.mult)
            step(w.tensor_copy(ke[:, NL], kj))
            dve.sem_inc(to_pe, 1)
            dve.wait_ge(from_pe, 1)
            for n in range(2):
                w.tensor_tensor(am[:, 2 * n:2 * n + 2], p_a[n][0:TS, 0:2 * (NL + 1) * TS].rearrange(
                    "p (h l t) -> p h l t", h=2, t=TS), bc(mask[:], 1, 2), ALU.mult)
            step(w.tensor_copy(kdT[:], p_t[0:TS, 0:2 * P]))
            dve.sem_inc(to_pe, 1)
            last = eb[:].rearrange("p c (b t) -> p c b t", t=NT)[:, :, :, NT - 1]
            step(w.tensor_tensor(std[:], st[:], bc(last, 3, HD), ALU.mult))
            dve.wait_ge(from_pe, 2)
            step(w.tensor_copy(oi[:], p_i[:, 0:2 * TS].rearrange("p (c t) -> p c t", c=2)))
            step(w.tensor_tensor(o[:], p_j[:, 0:2 * TS].rearrange("p (c t) -> p c t", c=2), oi[:], ALU.add))
            step(w.tensor_tensor(sq[:], o[:], o[:], ALU.mult))
            dve.sem_inc(to_pe, 1)
            step(w.tensor_tensor(st[:], std[:], p_u[:].rearrange("p c (b v) -> p c b v", v=HD), ALU.add))
            dve.sem_inc(done, 1)
            dve.wait_ge(from_act, 2)
            step(w.tensor_tensor(o[:], o[:], eb[:], ALU.mult))
            step(w.tensor_tensor(o[:], o[:], z[:, 2], ALU.mult))
            dve.sem_inc(done, 1)

        @block.tensor
        def _(pe):
            mm = nc.tensor.matmul
            pe.wait_ge(to_pe, 1)
            for c in range(2):
                nc.tensor.transpose(p_t[0:TS, c * P:(c + 1) * P], ex[:, NL, c, :], K["ident"][:])
            for n in range(NH):
                c, h = n // 2, HD * (n % 2)
                for l in range(NL + 1):
                    o0 = ((n // 2) * (NL + 1) + l) * TS
                    last = mm(p_a[n % 2][0:TS, o0:o0 + TS], ke[h:h + HD, l, c, :], qe[h:h + HD, l, c, :], start=True,
                              stop=True)
            last.then_inc(from_pe, 1)
            pe.wait_ge(to_pe, 2)
            for n in range(NH):
                c, h = n // 2, HD * (n % 2)
                for l in range(NL + 1):
                    mm(p_i[h:h + HD, c * TS:(c + 1) * TS], v[:, n * HD:(n + 1) * HD], am[:, 2 * (n % 2) + c, l, :],
                       start=(l == 0), stop=(l == NL))
                for k in range(NB):
                    mm(p_j[h:h + HD, c * TS + k * NT:c * TS + (k + 1) * NT], st[h:h + HD, c, k, :],
                       qb[h:h + HD, c, k * NT:(k + 1) * NT], start=True, stop=True)
                last = mm(p_u[h:h + HD, c, :].rearrange("p (b v) -> p b v", v=HD), kdT[:, n * HD:(n + 1) * HD],
                          vm[:, :, n * HD:(n + 1) * HD], start=True, stop=True)
            last.then_inc(from_pe, 1)
            pe.wait_ge(to_pe, 3)
            mm(p_r[:, 0:2 * TS], K["pairones"][:], sq[:].rearrange("p c t -> p (c t)"), start=True,
               stop=True).then_inc(from_pe, 1)


def stage_mix(nc, I, O, S, K):
    stage_residual(nc, I, O, S, K, "mix", "w_out", 8, None,
                   lambda tile, prompt: I["x_prompt"][tile, :] if prompt else I["x_sample"],
                   lambda tile, prompt: S["x1"][tile, :], 1, 2, mix=True, wq=True)


def stage_cross_out(nc, I, O, S, K):
    stage_residual(nc, I, O, S, K, "cross", "xa_wo", 2, S["xa_o"],
                   lambda tile, prompt: S["x1"][tile, :], lambda tile, prompt: S["x2"][tile, :], 3, 4, keep_h=True)


INS = {
    "x_prompt": (L, D), "mem_prompt": (MEM, D), "x_sample": (TS, D),
    "cache_fox_kv": (160, PAGE, 2 * GW), "cache_fox_logf": (160, PAGE, NH), "cache_nsa_kv": (160, PAGE, 4 * HD),
    "state_nsa_win": (NB, WIN, 2 * HD), "state_hgrn": (NB, NH, HD, HD), "state_lru_h": (NB, GW),
    "state_lru_conv": (NB, 3, GW), "cache_xa_kv": (NB, MEM, 2 * GW), "page_table": (1, NB * NPAGE),
    "w_in": (D, C_END), "b_fox_f": (NH,), "hgrn_lower": (GW,), "nsa_cmp_w": (2, 32, HD), "lru_conv_w": (4, GW),
    "lru_conv_b": (GW,), "lru_wa": (4, HD, HD), "lru_ba": (GW,), "lru_wx": (4, HD, HD), "lru_bx": (GW,),
    "lru_lambda": (GW,), "g_mix": (D,), "w_out": (D, D), "g_mem": (D,), "xa_wq": (D, GW), "xa_wkv": (D, 2 * GW),
    "xa_wo": (GW, D), "w_ff1": (D, FF), "w_ff2": (FF, D), "norms": (6, D),
}
OUTS = [
    ("y_prompt", (L, D), (1, L, D)), ("y_sample", (TS, D), (NB, NT, D)),
    ("fox_kv_p", (L, 512), (1, 1, L, 2, NH, HD)), ("fox_logf_p", (L, NH), (1, 1, L, NH)),
    ("nsa_kv_p", (L, 256), (1, 1, L, 4, HD)), ("nsa_win_p", (WIN, 128), (1, 1, WIN, 2, HD)),
    ("hgrn_p", (NH, HD, HD), (1, 1, NH, HD, HD)), ("lru_h_p", (GW,), (1, 1, GW)),
    ("lru_conv_p", (3, GW), (1, 1, 3, GW)), ("xa_kv_p", (MEM, 512), (1, 1, MEM, 2, NH, HD)),
    ("fox_kv_s", (TS, 512), (1, NB, NT, 2, NH, HD)), ("fox_logf_s", (TS, NH), (1, NB, NT, NH)),
    ("nsa_kv_s", (TS, 256), (1, NB, NT, 4, HD)), ("nsa_win_s", (NB, WIN, 128), (1, NB, WIN, 2, HD)),
    ("hgrn_s", (NB, NH, HD, HD), (1, NB, NH, HD, HD)), ("lru_h_s", (NB, GW), (1, NB, GW)),
    ("lru_conv_s", (NB, 3, GW), (1, NB, 3, GW)),
]
SCRATCH = {
    "feat": (R_END, T), "hgrn_v": (T, GW), "win_kv": (T, 2 * HD), "group": (G_END, T), "sel_bias": (32, L),
    "x1": (T, D), "x2": (T, D), "h3": (D, T), "xa_k": (GW, MEM), "xa_q": (GW, T), "xa_o": (GW, T), "ff": (FF, T), "ff_part": (T, D), "gates": (16, T), "keyc": (NH, L),
    "lf_rows": (NB, NPAGE * PAGE * NH), "lf_sums": (NB, NH, PAST),
}
STAGES = [stage_project, stage_gates, stage_select, stage_fox, stage_sel, stage_win, stage_hgrn, stage_lru,
          stage_sample_fox, stage_sample_sel, stage_sample_win, stage_sample_hgrn, stage_memory, stage_mix,
          stage_cross, stage_sample_xa, stage_cross_out, stage_ff1, stage_ff2]


def program(nc, I, O, S, stages):
    with ExitStack() as ctx:
        K = {}
        Room.zeroed = []
        for n in ("ident", "ones", "pairones", "tri_kq", "tri_qk", "low_kq", "low_qk"):
            K[n] = ctx.enter_context(nc.sbuf_tensor(n, [P, P], F32))
        K["eps"] = ctx.enter_context(nc.sbuf_tensor("eps", [P, 1], F32))
        stage_constants(nc, K)
        for stage in stages:
            stage(nc, I, O, S, K)


def kernel(**inputs):
    import numpy as np
    import concourse.bacc as bacc
    from concourse.bass_utils import run_bass_kernel_spmd

    nc = bacc.Bacc("TRN2", target_bir_lowering=False, num_devices=1)
    arrays, I, O, S = {}, {}, {}, {}
    for name, shape in INS.items():
        a = np.ascontiguousarray(inputs[name]).reshape(shape)
        arrays[f"in_{name}"] = a
        I[name] = nc.dram_tensor(f"in_{name}", a.shape, mybir.dt.from_np(a.dtype), kind="ExternalInput").ap()
    for name, shape, _ in OUTS:
        O[name] = nc.dram_tensor(f"out_{name}", shape, F32, kind="ExternalOutput").ap()
    for name, shape in SCRATCH.items():
        S[name] = nc.dram_tensor(f"scratch_{name}", shape, F32, kind="Internal").ap()
    program(nc, I, O, S, STAGES)
    r = run_bass_kernel_spmd(nc, [arrays], core_ids=[0])
    return tuple(np.asarray(r.results[0][f"out_{name}"]).reshape(shape) for name, _, shape in OUTS)
```
